# Optimizing a Trainium2 kernel written in Bass

```python
import math, functools
import jax, jax.numpy as jnp
from jax import lax
import numpy as np
import math
import jax
import jax.numpy as jnp

D_MODEL = 1024
BATCH = 1
SEQ = 256
DEPTH = 2

GRID_W = 64
CTX_LEN = 256
N_MIXERS = 2
N_A_LAYERS = (DEPTH + 1) // 2
N_B_LAYERS = DEPTH // 2
D_FF = 2816
N_MOD = 9
EPS = 1e-6
ROPE_BASE = 10000.0
Q_BLOCK = 128
NEG_INF = -1e30

A_HEADS = 8
A_HEAD_DIM = 64
A_V_DIM = 2 * A_HEAD_DIM
A_QKV_COLS = 3 * A_HEADS * A_V_DIM
A_WIDTH = A_HEADS * A_V_DIM

B_Q_HEADS = 16
B_KV_HEADS = 4
B_HEAD_DIM = 64
B_GROUP = B_Q_HEADS // B_KV_HEADS
B_QKV_COLS = (B_Q_HEADS + 2 * B_KV_HEADS) * B_HEAD_DIM
B_WIDTH = B_Q_HEADS * B_HEAD_DIM
WINDOW = 128
BAND_BLOCK = 128


def rms(x):
    xf = x.astype(jnp.float32)
    return (xf * lax.rsqrt(jnp.mean(xf * xf, axis=-1, keepdims=True) + EPS)).astype(x.dtype)

def rms_gain(x, g):
    return rms(x) * g

def modulate(h, shift, scale):
    return h * (1 + scale) + shift

def swiglu(h, wi, wo):
    g, u = jnp.split(h @ wi, 2, axis=-1)
    return (jax.nn.silu(g) * u) @ wo

def axial_rope_tables(rows, head_dim):
    nf = head_dim // 4
    inv = ROPE_BASE ** (-jnp.arange(nf, dtype=jnp.float32) / nf)
    row = jnp.broadcast_to(jnp.arange(rows, dtype=jnp.float32)[:, None], (rows, GRID_W)).reshape(-1)
    col = jnp.broadcast_to(jnp.arange(GRID_W, dtype=jnp.float32)[None, :], (rows, GRID_W)).reshape(-1)
    ang = jnp.stack([row[:, None] * inv, col[:, None] * inv], axis=1)
    ang = jnp.stack([ang, ang], axis=2).reshape(rows * GRID_W, head_dim)
    return jnp.cos(ang), jnp.sin(ang)

def apply_rope(x, cos, sin):
    dh = x.shape[-1]
    xr = x.reshape(x.shape[:-1] + (2, 2, dh // 4))
    rot = jnp.stack([-xr[..., 1, :], xr[..., 0, :]], axis=-2).reshape(x.shape)
    return (x * cos + rot * sin).astype(x.dtype)

def diff_attention(h_lat, h_ctx, w_qkv, w_o, q_gain, k_gain, lam_vec, subln_gain, lam_init, cos, sin, ctx_out):
    B, L, _ = h_lat.shape

    def project(h):
        q, k, v = jnp.split(h @ w_qkv, [A_WIDTH, 2 * A_WIDTH], axis=-1)
        q = rms_gain(q.reshape(B, -1, A_HEADS, 2, A_HEAD_DIM), q_gain)
        k = rms_gain(k.reshape(B, -1, A_HEADS, 2, A_HEAD_DIM), k_gain)
        return q, k, v.reshape(B, -1, A_HEADS, A_V_DIM)

    q_l, k_l, v_l = project(h_lat)
    q_c, k_c, v_c = project(h_ctx)
    rc, rs = cos[:, None, None, :], sin[:, None, None, :]
    q_l, k_l = apply_rope(q_l, rc, rs), apply_rope(k_l, rc, rs)

    lv = lam_vec.astype(jnp.float32)
    lam = jnp.exp(jnp.sum(lv[0] * lv[1])) - jnp.exp(jnp.sum(lv[2] * lv[3])) + lam_init
    scale = A_HEAD_DIM ** -0.5

    def attend(q, k, v):
        s = jnp.einsum('bqhcd,bkhcd->bhcqk', q, k).astype(jnp.float32) * scale
        p = jax.nn.softmax(s, axis=-1)
        a = (p[:, :, 0] - lam * p[:, :, 1]).astype(v.dtype)
        return jnp.einsum('bhqk,bkhe->bqhe', a, v)

    def finish(o):
        o = rms_gain(o, subln_gain) * (1.0 - lam_init)
        return o.reshape(o.shape[0], o.shape[1], A_WIDTH) @ w_o

    k_all = jnp.concatenate([k_l, k_c], axis=1)
    v_all = jnp.concatenate([v_l, v_c], axis=1)
    nb = L // Q_BLOCK
    qb = q_l.reshape(B, nb, Q_BLOCK, A_HEADS, 2, A_HEAD_DIM).transpose(1, 0, 2, 3, 4, 5)
    o_l = lax.map(lambda qblk: attend(qblk, k_all, v_all), qb)
    o_l = o_l.transpose(1, 0, 2, 3, 4).reshape(B, L, A_HEADS, A_V_DIM)
    out_l = finish(o_l)
    out_c = finish(attend(q_c, k_c, v_c)) if ctx_out else None
    return out_l, out_c

def window_gqa(h_lat, h_ctx, w_qkv, w_o, q_gain, k_gain, sink, cos, sin, ctx_out):
    B, L, _ = h_lat.shape
    nb = L // BAND_BLOCK
    BB = BAND_BLOCK

    def project(h):
        q, k, v = jnp.split(h @ w_qkv, [B_WIDTH, B_WIDTH + B_KV_HEADS * B_HEAD_DIM], axis=-1)
        q = rms_gain(q.reshape(B, -1, B_KV_HEADS, B_GROUP, B_HEAD_DIM), q_gain)
        k = rms_gain(k.reshape(B, -1, B_KV_HEADS, B_HEAD_DIM), k_gain)
        return q, k, v.reshape(B, -1, B_KV_HEADS, B_HEAD_DIM)

    q_l, k_l, v_l = project(h_lat)
    q_c, k_c, v_c = project(h_ctx)
    q_l = apply_rope(q_l, cos[:, None, None, :], sin[:, None, None, :])
    k_l = apply_rope(k_l, cos[:, None, :], sin[:, None, :])
    scale = B_HEAD_DIM ** -0.5
    sink_f = sink.astype(jnp.float32).reshape(B_KV_HEADS, B_GROUP)

    def band(t):
        tb = jnp.pad(t, ((0, 0), (BB, BB), (0, 0), (0, 0))).reshape(B, nb + 2, BB, B_KV_HEADS, B_HEAD_DIM)
        return jnp.concatenate([tb[:, :-2], tb[:, 1:-1], tb[:, 2:]], axis=2)

    k_w, v_w = band(k_l), band(v_l)
    qb = q_l.reshape(B, nb, BB, B_KV_HEADS, B_GROUP, B_HEAD_DIM)
    s_w = jnp.einsum('bnqhgd,bnkhd->bnhgqk', qb, k_w).astype(jnp.float32) * scale
    s_c = jnp.einsum('bnqhgd,bkhd->bnhgqk', qb, k_c).astype(jnp.float32) * scale
    qi = jnp.arange(BB)
    kj = jnp.arange(3 * BB)
    rel = kj[None, :] - BB - qi[:, None]
    kpos = jnp.arange(nb)[:, None] * BB - BB + kj[None, :]
    valid = (jnp.abs(rel) <= WINDOW)[None] & ((kpos >= 0) & (kpos < L))[:, None, :]
    s_w = jnp.where(valid[None, :, None, None], s_w, NEG_INF)
    sink_b = jnp.broadcast_to(sink_f[None, None, :, :, None, None], s_w.shape[:-1] + (1,))
    n_ctx = k_c.shape[1]
    p = jax.nn.softmax(jnp.concatenate([s_w, s_c, sink_b], axis=-1), axis=-1)
    p_w = p[..., :3 * BB].astype(v_w.dtype)
    p_c = p[..., 3 * BB:3 * BB + n_ctx].astype(v_c.dtype)
    o = jnp.einsum('bnhgqk,bnkhd->bnqhgd', p_w, v_w) + jnp.einsum('bnhgqk,bkhd->bnqhgd', p_c, v_c)
    out_l = o.reshape(B, L, B_WIDTH) @ w_o
    out_c = None
    if ctx_out:
        s = jnp.einsum('bqhgd,bkhd->bhgqk', q_c, k_c).astype(jnp.float32) * scale
        sb = jnp.broadcast_to(sink_f[None, :, :, None, None], s.shape[:-1] + (1,))
        pc = jax.nn.softmax(jnp.concatenate([s, sb], axis=-1), axis=-1)[..., :n_ctx].astype(v_c.dtype)
        oc = jnp.einsum('bhgqk,bkhd->bqhgd', pc, v_c)
        out_c = oc.reshape(B, n_ctx, B_WIDTH) @ w_o
    return out_l, out_c

def layer(x, xc, mod_l, mod_c, pre_wi, pre_wo, post_wi, post_wo, mixer, ctx_out):
    sh1, sc1, g1, sh2, sc2, g2, sh3, sc3, g3 = jnp.split(mod_l, N_MOD, axis=-1)
    ch1, cc1, cg1, ch2, cc2, cg2, ch3, cc3, cg3 = jnp.split(mod_c, N_MOD, axis=-1)

    def ffn_step(t, sh, sc, g, wi, wo):
        return t + 0.5 * g * swiglu(modulate(rms(t), sh, sc), wi, wo)

    x = ffn_step(x, sh1, sc1, g1, pre_wi, pre_wo)
    xc = ffn_step(xc, ch1, cc1, cg1, pre_wi, pre_wo)
    o_l, o_c = mixer(h_lat=modulate(rms(x), sh2, sc2), h_ctx=modulate(rms(xc), ch2, cc2), ctx_out=ctx_out)
    x = x + g2 * o_l
    x = ffn_step(x, sh3, sc3, g3, post_wi, post_wo)
    if ctx_out:
        xc = xc + cg2 * o_c
        xc = ffn_step(xc, ch3, cc3, cg3, post_wi, post_wo)
    return x, xc

def first_inputs(seed: int = 0) -> dict:
    key = jax.random.key(seed)
    ks = jax.random.split(key, 24)
    f32 = jnp.float32
    D = D_MODEL

    def nrm(k, shape, s):
        return jax.random.normal(k, shape, f32) * s

    return {
        "x": nrm(ks[0], (BATCH, SEQ, D), 1.0),
        "c": nrm(ks[1], (BATCH, D), 1.0),
        "ctx": nrm(ks[2], (BATCH, CTX_LEN, D), 1.0),
        "c_ctx": nrm(ks[3], (D,), 1.0),
        "ada_w": nrm(ks[4], (DEPTH, D, N_MOD * D), 0.5 * D ** -0.5),
        "ada_b": nrm(ks[5], (DEPTH, N_MOD * D), 0.02),
        "ffn_pre_wi": nrm(ks[6], (DEPTH, D, 2 * D_FF), D ** -0.5),
        "ffn_pre_wo": nrm(ks[7], (DEPTH, D_FF, D), D_FF ** -0.5),
        "ffn_post_wi": nrm(ks[8], (DEPTH, D, 2 * D_FF), D ** -0.5),
        "ffn_post_wo": nrm(ks[9], (DEPTH, D_FF, D), D_FF ** -0.5),
        "a_w_qkv": nrm(ks[10], (N_A_LAYERS, D, A_QKV_COLS), D ** -0.5),
        "a_w_o": nrm(ks[11], (N_A_LAYERS, A_WIDTH, D), A_WIDTH ** -0.5),
        "a_q_gain": 1.0 + nrm(ks[12], (N_A_LAYERS, A_HEAD_DIM), 0.1),
        "a_k_gain": 1.0 + nrm(ks[13], (N_A_LAYERS, A_HEAD_DIM), 0.1),
        "a_lambda": nrm(ks[14], (N_A_LAYERS, 4, A_HEAD_DIM), 0.1),
        "a_subln_gain": 1.0 + nrm(ks[15], (N_A_LAYERS, A_V_DIM), 0.1),
        "b_w_qkv": nrm(ks[16], (N_B_LAYERS, D, B_QKV_COLS), D ** -0.5),
        "b_w_o": nrm(ks[17], (N_B_LAYERS, B_WIDTH, D), B_WIDTH ** -0.5),
        "b_q_gain": 1.0 + nrm(ks[18], (N_B_LAYERS, B_HEAD_DIM), 0.1),
        "b_k_gain": 1.0 + nrm(ks[19], (N_B_LAYERS, B_HEAD_DIM), 0.1),
        "b_sink": nrm(ks[20], (N_B_LAYERS, B_Q_HEADS), 0.5),
    }

def first_block(x, c, ctx, c_ctx, ada_w, ada_b, ffn_pre_wi, ffn_pre_wo, ffn_post_wi, ffn_post_wo,
              a_w_qkv, a_w_o, a_q_gain, a_k_gain, a_lambda, a_subln_gain,
              b_w_qkv, b_w_o, b_q_gain, b_k_gain, b_sink):
    n_tok = x.shape[1]
    rows = n_tok // GRID_W
    cos, sin = axial_rope_tables(rows, A_HEAD_DIM)
    xc = ctx
    for i in range(DEPTH):
        mod_l = (jax.nn.silu(c) @ ada_w[i] + ada_b[i])[:, None, :]
        mod_c = jax.nn.silu(c_ctx) @ ada_w[i] + ada_b[i]
        ctx_out = i < DEPTH - 1
        j = i // N_MIXERS
        if i % N_MIXERS == 0:
            mixer = functools.partial(diff_attention, w_qkv=a_w_qkv[j], w_o=a_w_o[j], q_gain=a_q_gain[j],
                                      k_gain=a_k_gain[j], lam_vec=a_lambda[j], subln_gain=a_subln_gain[j],
                                      lam_init=0.8 - 0.6 * math.exp(-0.3 * i), cos=cos, sin=sin)
        else:
            mixer = functools.partial(window_gqa, w_qkv=b_w_qkv[j], w_o=b_w_o[j], q_gain=b_q_gain[j],
                                      k_gain=b_k_gain[j], sink=b_sink[j], cos=cos, sin=sin)
        x, xc = layer(x, xc, mod_l, mod_c, ffn_pre_wi[i], ffn_pre_wo[i], ffn_post_wi[i], ffn_post_wo[i],
                      mixer, ctx_out)
    return x


DEPTH_2 = 1

N_HEADS_DIL = 6
N_HEADS_MOBA = 6
N_HEADS_MEM = 4
N_HEADS_MIX = N_HEADS_DIL + N_HEADS_MOBA + N_HEADS_MEM
HEAD_DIM = D_MODEL // N_HEADS_MIX
W_DIL = N_HEADS_DIL * HEAD_DIM
W_MOBA = N_HEADS_MOBA * HEAD_DIM
W_MEM = N_HEADS_MEM * HEAD_DIM
MIX_WIDTH = W_DIL + W_MOBA + W_MEM
IN_WIDTH = 3 * W_DIL + 3 * W_MOBA + W_MEM
DIL_CONFIGS = ((128, 1), (512, 4), (2048, 16))
MOBA_BLOCK = 256
MOBA_TOPK = 3
MOBA_QBLOCK = 128
MEM_LEN = 256
PEER_HEADS = 8
PEER_NKEYS = 128
PEER_EXPERTS = PEER_NKEYS * PEER_NKEYS
PEER_TOPK = 16
PEER_DKEY = 256
PEER_CHUNK = 128
RMS_EPS = 1e-6
NEG_INF_2 = -1e30


def rms_norm(a, g):
    af = a.astype(jnp.float32)
    y = af * lax.rsqrt(jnp.mean(af * af, axis=-1, keepdims=True) + RMS_EPS)
    return (y * g.astype(jnp.float32)).astype(a.dtype)

def split_heads(a, n_heads):
    b, s, _ = a.shape
    return a.reshape(b, s, n_heads, HEAD_DIM).transpose(0, 2, 1, 3)

def merge_heads(a):
    b, h, s, dh = a.shape
    return a.transpose(0, 2, 1, 3).reshape(b, s, h * dh)

def alibi_slopes(n):
    return jnp.exp2(-8.0 * jnp.arange(1, n + 1, dtype=jnp.float32) / n)

def dilated_branch(q, k, v, slopes, window, dilation):
    B, H, S, Dh = q.shape
    L = S // dilation
    n_blk = -(-L // BAND_BLOCK)
    Lp = n_blk * BAND_BLOCK
    reach = window // dilation

    def split(a):
        a = a.reshape(B, H, L, dilation, Dh).transpose(0, 1, 3, 2, 4)
        a = jnp.pad(a, ((0, 0), (0, 0), (0, 0), (0, Lp - L), (0, 0)))
        return a.reshape(B, H, dilation, n_blk, BAND_BLOCK, Dh)

    def with_prev(a):
        prev = jnp.pad(a, ((0, 0), (0, 0), (0, 0), (1, 0), (0, 0), (0, 0)))[:, :, :, :-1]
        return jnp.concatenate([prev, a], axis=4)

    qb = split(q)
    kc = with_prev(split(k))
    vc = with_prev(split(v))
    s = jnp.einsum('bhrnqd,bhrnkd->bhrnqk', qb, kc).astype(jnp.float32) * (1.0 / math.sqrt(Dh))
    ql = jnp.arange(BAND_BLOCK)[:, None]
    kl = jnp.arange(2 * BAND_BLOCK)[None, :]
    delta = BAND_BLOCK + ql - kl
    blk = jnp.arange(n_blk)[:, None, None]
    valid = (delta >= 0) & (delta <= reach) & (blk * BAND_BLOCK - BAND_BLOCK + kl[None] >= 0)
    bias = -slopes[:, None, None, None, None] * (delta * dilation).astype(jnp.float32)
    s = jnp.where(valid, s + bias, NEG_INF_2)
    m = jnp.max(s, axis=-1, keepdims=True)
    p = jnp.exp(s - m)
    den = jnp.sum(p, axis=-1, keepdims=True)
    lse = m[..., 0] + jnp.log(den[..., 0])
    o = jnp.einsum('bhrnqk,bhrnkd->bhrnqd', p.astype(v.dtype), vc) / den.astype(v.dtype)

    def merge(a):
        tail = a.shape[5:]
        a = a.reshape((B, H, dilation, Lp) + tail)[:, :, :, :L]
        a = jnp.moveaxis(a, 2, 3)
        return a.reshape((B, H, S) + tail)

    return merge(o), merge(lse)

def dilated_mixture(q, k, v, slopes):
    outs, lses = [], []
    for window, dilation in DIL_CONFIGS:
        o, l = dilated_branch(q, k, v, slopes, window, dilation)
        outs.append(o)
        lses.append(l)
    wts = jax.nn.softmax(jnp.stack(lses, axis=0), axis=0).astype(q.dtype)
    return jnp.einsum('cbhs,cbhsd->bhsd', wts, jnp.stack(outs, axis=0))

def moba_attention(q, k, v, slopes):
    B, H, S, Dh = q.shape
    n_blk = -(-S // MOBA_BLOCK)
    Sp = n_blk * MOBA_BLOCK
    pad = ((0, 0), (0, 0), (0, Sp - S), (0, 0))
    kb = jnp.pad(k, pad).reshape(B, H, n_blk, MOBA_BLOCK, Dh)
    vb = jnp.pad(v, pad).reshape(B, H, n_blk, MOBA_BLOCK, Dh)
    k_mean = jnp.mean(kb.astype(jnp.float32), axis=3).astype(k.dtype)
    gate = jnp.einsum('bhsd,bhnd->bhsn', q, k_mean).astype(jnp.float32)
    n_past = jnp.arange(S) // MOBA_BLOCK
    past = jnp.arange(n_blk)[None, :] < n_past[:, None]
    gate = jnp.where(past, gate, NEG_INF_2)
    k_sel = min(MOBA_TOPK, n_blk)
    _, sel = lax.top_k(gate, k_sel)

    n_qb = S // MOBA_QBLOCK
    qq = q.reshape(B, H, n_qb, MOBA_QBLOCK, Dh).transpose(0, 2, 1, 3, 4).reshape(B * n_qb, H, MOBA_QBLOCK, Dh)
    ss = sel.reshape(B, H, n_qb, MOBA_QBLOCK, k_sel).transpose(0, 2, 1, 3, 4).reshape(B * n_qb, H, MOBA_QBLOCK, k_sel)
    b_ids = jnp.repeat(jnp.arange(B, dtype=jnp.int32), n_qb)
    n_ids = jnp.tile(jnp.arange(n_qb, dtype=jnp.int32), B)
    head = jnp.arange(H)[:, None, None]
    scale = 1.0 / math.sqrt(Dh)
    n_sel_keys = k_sel * MOBA_BLOCK

    def step(args):
        q_blk, sel_blk, b, n = args
        kb_b = lax.dynamic_index_in_dim(kb, b, axis=0, keepdims=False)
        vb_b = lax.dynamic_index_in_dim(vb, b, axis=0, keepdims=False)
        t_q = n * MOBA_QBLOCK + jnp.arange(MOBA_QBLOCK)
        k_g = kb_b[head, sel_blk]
        v_g = vb_b[head, sel_blk]
        s_sel = jnp.einsum('hqd,hqjkd->hqjk', q_blk, k_g).astype(jnp.float32) * scale
        s_pos = sel_blk[..., None] * MOBA_BLOCK + jnp.arange(MOBA_BLOCK)
        ok = jnp.arange(k_sel)[None, :] < (t_q // MOBA_BLOCK)[:, None]
        dist_sel = (t_q[None, :, None, None] - s_pos).astype(jnp.float32)
        s_sel = jnp.where(ok[None, :, :, None], s_sel - slopes[:, None, None, None] * dist_sel, NEG_INF_2)
        own = (n * MOBA_QBLOCK) // MOBA_BLOCK
        k_own = lax.dynamic_index_in_dim(kb_b, own, axis=1, keepdims=False)
        v_own = lax.dynamic_index_in_dim(vb_b, own, axis=1, keepdims=False)
        o_pos = own * MOBA_BLOCK + jnp.arange(MOBA_BLOCK)
        dist_own = t_q[:, None] - o_pos[None, :]
        s_own = jnp.einsum('hqd,hkd->hqk', q_blk, k_own).astype(jnp.float32) * scale
        s_own = jnp.where(dist_own >= 0, s_own - slopes[:, None, None] * dist_own.astype(jnp.float32), NEG_INF_2)
        s_all = jnp.concatenate([s_sel.reshape(H, MOBA_QBLOCK, n_sel_keys), s_own], axis=-1)
        p = jax.nn.softmax(s_all, axis=-1).astype(v.dtype)
        p_sel = p[..., :n_sel_keys].reshape(H, MOBA_QBLOCK, k_sel, MOBA_BLOCK)
        p_own = p[..., n_sel_keys:]
        return (jnp.einsum('hqjk,hqjkd->hqd', p_sel, v_g)
                + jnp.einsum('hqk,hkd->hqd', p_own, v_own))

    out = lax.map(step, (qq, ss, b_ids, n_ids))
    return out.reshape(B, n_qb, H, MOBA_QBLOCK, Dh).transpose(0, 2, 1, 3, 4).reshape(B, H, S, Dh)

def memory_attention(q, k, v):
    s = jnp.einsum('bhsd,bhmd->bhsm', q, k).astype(jnp.float32) * (1.0 / math.sqrt(q.shape[-1]))
    p = jax.nn.softmax(s, axis=-1).astype(v.dtype)
    return jnp.einsum('bhsm,bhmd->bhsd', p, v)

def peer_ffn(h, w_q, sub1, sub2, u, v):
    B, S, D = h.shape
    half = PEER_DKEY // 2
    qry = (h @ w_q).reshape(B, S, PEER_HEADS, PEER_DKEY)
    s1 = jnp.einsum('bshd,hkd->bshk', qry[..., :half], sub1).astype(jnp.float32)
    s2 = jnp.einsum('bshd,hkd->bshk', qry[..., half:], sub2).astype(jnp.float32)
    v1, i1 = lax.top_k(s1, PEER_TOPK)
    v2, i2 = lax.top_k(s2, PEER_TOPK)
    cand = (v1[..., :, None] + v2[..., None, :]).reshape(B, S, PEER_HEADS, PEER_TOPK * PEER_TOPK)
    cand_idx = (i1[..., :, None] * PEER_NKEYS + i2[..., None, :]).reshape(B, S, PEER_HEADS, PEER_TOPK * PEER_TOPK)
    top_s, pos = lax.top_k(cand, PEER_TOPK)
    expert = jnp.take_along_axis(cand_idx, pos, axis=-1)
    gate = jax.nn.softmax(top_s, axis=-1)
    T = B * S
    E = PEER_HEADS * PEER_TOPK
    n_chunk = T // PEER_CHUNK
    hx = h.reshape(n_chunk, PEER_CHUNK, D)
    ex = expert.reshape(n_chunk, PEER_CHUNK, E)
    gx = gate.reshape(n_chunk, PEER_CHUNK, E).astype(h.dtype)

    def step(args):
        x_c, e_c, g_c = args
        a = jnp.einsum('cd,ced->ce', x_c, u[e_c])
        w = jax.nn.gelu(a.astype(jnp.float32), approximate=False).astype(x_c.dtype) * g_c
        return jnp.einsum('ce,ced->cd', w, v[e_c])

    return lax.map(step, (hx, ex, gx)).reshape(B, S, D)

def hybrid_layer(x, mem, g_mix, w_in, qg_dil, kg_dil, qg_moba, kg_moba, qg_mem, kg_mem, g_memtok, w_mem_kv,
                 og_dil, og_moba, og_mem, w_out, g_ffn, w_peer_q, sub1, sub2, peer_u, peer_v):
    slopes = alibi_slopes(N_HEADS_DIL + N_HEADS_MOBA)
    sl_dil, sl_moba = slopes[0::2], slopes[1::2]
    hn = rms_norm(x, g_mix)
    proj = hn @ w_in
    cuts = [W_DIL, 2 * W_DIL, 3 * W_DIL, 3 * W_DIL + W_MOBA, 3 * W_DIL + 2 * W_MOBA, 3 * W_DIL + 3 * W_MOBA]
    q_d, k_d, v_d, q_b, k_b, v_b, q_m = jnp.split(proj, cuts, axis=-1)
    q_d = rms_norm(split_heads(q_d, N_HEADS_DIL), qg_dil)
    k_d = rms_norm(split_heads(k_d, N_HEADS_DIL), kg_dil)
    o_dil = dilated_mixture(q_d, k_d, split_heads(v_d, N_HEADS_DIL), sl_dil)
    q_b = rms_norm(split_heads(q_b, N_HEADS_MOBA), qg_moba)
    k_b = rms_norm(split_heads(k_b, N_HEADS_MOBA), kg_moba)
    o_moba = moba_attention(q_b, k_b, split_heads(v_b, N_HEADS_MOBA), sl_moba)
    kv = rms_norm(mem, g_memtok) @ w_mem_kv
    k_m, v_m = jnp.split(kv, 2, axis=-1)
    q_m = rms_norm(split_heads(q_m, N_HEADS_MEM), qg_mem)
    k_m = rms_norm(split_heads(k_m, N_HEADS_MEM), kg_mem)
    o_mem = memory_attention(q_m, k_m, split_heads(v_m, N_HEADS_MEM))
    y = jnp.concatenate([rms_norm(merge_heads(o_dil), og_dil),
                         rms_norm(merge_heads(o_moba), og_moba),
                         rms_norm(merge_heads(o_mem), og_mem)], axis=-1) @ w_out
    x = x + y
    x = x + peer_ffn(rms_norm(x, g_ffn), w_peer_q, sub1, sub2, peer_u, peer_v)
    return x

def second_inputs(seed: int = 0) -> dict:
    key = jax.random.key(seed)
    ks = jax.random.split(key, 24)

    def nrm(k, shape, scale):
        return jax.random.normal(k, shape, jnp.float32) * scale

    def gain(k, n):
        return 1.0 + 0.02 * jax.random.normal(k, (DEPTH_2, n), jnp.float32)

    return {
        'x': nrm(ks[0], (BATCH, SEQ, D_MODEL), 1.0),
        'mem': nrm(ks[1], (BATCH, MEM_LEN, D_MODEL), 1.0),
        'g_mix': gain(ks[2], D_MODEL),
        'w_in': nrm(ks[3], (DEPTH_2, D_MODEL, IN_WIDTH), D_MODEL ** -0.5),
        'qg_dil': gain(ks[4], HEAD_DIM),
        'kg_dil': gain(ks[5], HEAD_DIM),
        'qg_moba': gain(ks[6], HEAD_DIM),
        'kg_moba': gain(ks[7], HEAD_DIM),
        'qg_mem': gain(ks[8], HEAD_DIM),
        'kg_mem': gain(ks[9], HEAD_DIM),
        'g_memtok': gain(ks[10], D_MODEL),
        'w_mem_kv': nrm(ks[11], (DEPTH_2, D_MODEL, 2 * W_MEM), D_MODEL ** -0.5),
        'og_dil': gain(ks[12], W_DIL),
        'og_moba': gain(ks[13], W_MOBA),
        'og_mem': gain(ks[14], W_MEM),
        'w_out': nrm(ks[15], (DEPTH_2, MIX_WIDTH, D_MODEL), MIX_WIDTH ** -0.5),
        'g_ffn': gain(ks[16], D_MODEL),
        'w_peer_q': nrm(ks[17], (DEPTH_2, D_MODEL, PEER_HEADS * PEER_DKEY), D_MODEL ** -0.5),
        'peer_subkeys_1': nrm(ks[18], (DEPTH_2, PEER_HEADS, PEER_NKEYS, PEER_DKEY // 2), (PEER_DKEY // 2) ** -0.5),
        'peer_subkeys_2': nrm(ks[19], (DEPTH_2, PEER_HEADS, PEER_NKEYS, PEER_DKEY // 2), (PEER_DKEY // 2) ** -0.5),
        'peer_u': nrm(ks[20], (DEPTH_2, PEER_EXPERTS, D_MODEL), D_MODEL ** -0.5),
        'peer_v': nrm(ks[21], (DEPTH_2, PEER_EXPERTS, D_MODEL), PEER_HEADS ** -0.5),
    }

def second_block(x, mem, g_mix, w_in, qg_dil, kg_dil, qg_moba, kg_moba, qg_mem, kg_mem, g_memtok, w_mem_kv,
              og_dil, og_moba, og_mem, w_out, g_ffn, w_peer_q, peer_subkeys_1, peer_subkeys_2, peer_u, peer_v):
    h = x
    for layer in range(DEPTH_2):
        h = hybrid_layer(h, mem, g_mix[layer], w_in[layer], qg_dil[layer], kg_dil[layer], qg_moba[layer],
                         kg_moba[layer], qg_mem[layer], kg_mem[layer], g_memtok[layer], w_mem_kv[layer],
                         og_dil[layer], og_moba[layer], og_mem[layer], w_out[layer], g_ffn[layer],
                         w_peer_q[layer], peer_subkeys_1[layer], peer_subkeys_2[layer], peer_u[layer],
                         peer_v[layer])
    return h


def setup_inputs(seed=0):
    out = dict(first_inputs(seed))
    for name, value in second_inputs(seed + 1).items():
        if name != "x":
            out[name + "_2"] = value
    return out


def reference(
    x, c, ctx, c_ctx, ada_w, ada_b, ffn_pre_wi, ffn_pre_wo, ffn_post_wi, ffn_post_wo, a_w_qkv,
    a_w_o, a_q_gain, a_k_gain, a_lambda, a_subln_gain, b_w_qkv, b_w_o, b_q_gain, b_k_gain,
    b_sink, mem_2, g_mix_2, w_in_2, qg_dil_2, kg_dil_2, qg_moba_2, kg_moba_2, qg_mem_2,
    kg_mem_2, g_memtok_2, w_mem_kv_2, og_dil_2, og_moba_2, og_mem_2, w_out_2, g_ffn_2,
    w_peer_q_2, peer_subkeys_1_2, peer_subkeys_2_2, peer_u_2, peer_v_2,
):
    x = first_block(
        x, c, ctx, c_ctx, ada_w, ada_b, ffn_pre_wi, ffn_pre_wo, ffn_post_wi, ffn_post_wo,
        a_w_qkv, a_w_o, a_q_gain, a_k_gain, a_lambda, a_subln_gain, b_w_qkv, b_w_o, b_q_gain,
        b_k_gain, b_sink,
    )
    return second_block(
        x, mem_2, g_mix_2, w_in_2, qg_dil_2, kg_dil_2, qg_moba_2, kg_moba_2, qg_mem_2, kg_mem_2,
        g_memtok_2, w_mem_kv_2, og_dil_2, og_moba_2, og_mem_2, w_out_2, g_ffn_2, w_peer_q_2,
        peer_subkeys_1_2, peer_subkeys_2_2, peer_u_2, peer_v_2,
    )


_drawn_inputs = setup_inputs


def setup_inputs(seed=0):
    import zlib

    import numpy as np

    out = dict(_drawn_inputs(seed))
    spreads = {}
    factors = {'a_q_gain': 2.822,
     'a_k_gain': 2.705,
     'b_q_gain': 7.103,
     'b_k_gain': 7.031,
     'b_sink': 8.0,
     'qg_dil_2': 5.651,
     'kg_dil_2': 5.344,
     'qg_moba_2': 5.583,
     'kg_moba_2': 5.316,
     'qg_mem_2': 4.609,
     'kg_mem_2': 4.853,
     'g_memtok_2': 3.481,
     'og_dil_2': 15.614,
     'og_moba_2': 15.169,
     'og_mem_2': 20.372,
     'g_ffn_2': 11.875}
    for name, (base, spread) in spreads.items():
        noise = np.random.default_rng([zlib.crc32(name.encode()), seed]).standard_normal(out[name].shape)
        drawn = base * np.exp(spread * noise) if base else spread * noise
        out[name] = jnp.asarray(drawn.astype(out[name].dtype))
    for name, factor in factors.items():
        out[name] = (out[name] * factor).astype(out[name].dtype)
    return out
```

```python
from contextlib import ExitStack

import concourse.bass as bass
from concourse import mybir

F32 = mybir.dt.float32
F32R = mybir.dt.float32r
U32 = mybir.dt.uint32
ACT = mybir.ActivationFunctionType
ALU = mybir.AluOpType
AX_X = mybir.AxisListType.X

P = 128
D = 1024
KC = D // P
NT = 256
HALVES = 2
FC = 22
WO_T = 3
R = 4
AHEAD = 3
HEAD = 64
EPS = 1e-6
NEG = -1.0e30
SCALE = HEAD ** -0.5
LAM_INIT = 0.2
N_MOD = 9
ADA_CHUNKS = N_MOD * KC
ADA_TILES = 4
ADA_PART = (12, 16, 8)
EXPERT_CHUNKS = 128
TOPK = 16
PEER_ROWS = 16
EARLY_CHUNKS = 40
TOKENS_PER_GROUP = 2

SMALL = {}
_at = 0
for _name, _n in (("a_q", 1), ("a_k", 1), ("a_sub", 1), ("b_q", 1), ("b_k", 1), ("dil_q", 1), ("dil_k", 1),
                  ("moba_q", 1), ("moba_k", 1), ("mem_q", 1), ("mem_k", 1), ("g_mix", KC), ("g_mem", KC),
                  ("og", KC), ("g_ffn", KC), ("one", 1), ("pick", 2 * KC - 1), ("sink", 16), ("lam", 4 * HEAD), ("c", 2 * KC),
                  ("ada_b", 2 * ADA_CHUNKS)):
    SMALL[_name] = (_at, _n)
    _at += _n
N_SMALL = _at


def stream_plan():
    at, first = 0, {}
    for name, n in (("ada0", ADA_TILES * ADA_PART[0]), ("wi0", 2 * FC), ("wo0", KC * WO_T), ("qkv_a", 24),
                    ("ada1", ADA_TILES * ADA_PART[1]), ("out_a", KC),
                    ("wi1", 2 * FC), ("wo1", KC * WO_T), ("wi2", 2 * FC), ("wo2", KC * WO_T),
                    ("qkv_b", 12), ("ada2", ADA_TILES * ADA_PART[2]), ("out_b", KC), ("wi3", 2 * FC), ("wo3", KC * WO_T),
                    ("proj_c", 24), ("out_c", KC), ("peer_q", PEER_ROWS), ("peer", 2 * EXPERT_CHUNKS)):
        assert at % R == 0 and n % R == 0
        first[name] = at
        at += n
    return first, at


FIRST, N_TILES = stream_plan()


def program(nc, w_stream, x_in, mem_in, small_in, const_in, rope_in, fan_in, mask_in, bias_in, sub_in, gelu_dram, out):
    with ExitStack() as ctx:
        def sb(name, shape, at, dt=F32):
            return nc.alloc_sbuf_tensor_at(name, shape, dt, offset=at)

        def sem(name):
            return ctx.enter_context(nc.semaphore(name))

        KB = 1024
        base = 1152
        raw = sb("raw", [P, R, D], base)
        w_hi = sb("w_hi", [P, R, D], base + 16 * KB, F32R)
        w_lo = sb("w_lo", [P, R, D], base + 32 * KB, F32R)
        X = sb("X", [P, HALVES, KC, NT], base + 48 * KB)
        H = sb("H", [P, HALVES, 2, KC, NT], base + 64 * KB, F32R)
        gates_at = base + 80 * KB
        arena = base + 96 * KB
        scratch = arena + 88 * KB
        act_hi = sb("act_hi", [P, FC, 2 * NT], arena, F32R)
        act_lo = sb("act_lo", [P, FC, 2 * NT], arena + 44 * KB, F32R)
        Q = sb("Q", [P, KC, 2 * NT], arena)
        K = sb("K", [P, KC, 2 * NT], arena + 16 * KB)
        V = sb("V", [P, 4, D], arena + 32 * KB)
        Qc = sb("Qc", [P, KC, NT], arena)
        Kc = sb("Kc", [P, KC, NT], arena + 8 * KB)
        Vc = sb("Vc", [P, 2, D], arena + 16 * KB)
        bias = sb("bias", [P, 12, 2, NT], arena + 24 * KB)
        pT = sb("pT", [P, 2, 2 * D], arena + 48 * KB)
        probs = sb("probs", [P, 3, 2, 512], arena + 64 * KB)
        logits = sb("logits", [P, 2, 2, 512], scratch)
        rope = sb("rope", [P, 2, 512], arena + 80 * KB)
        fan = sb("fan", [KC, KC, P], arena + 84 * KB)
        mask = sb("mask", [P, 2, 512], arena + 84 * KB)
        sub = sb("sub", [P, PEER_ROWS, P], arena)
        S = sb("S", [P, 2, PEER_ROWS, P], arena + 8 * KB)
        cand = sb("cand", [P, 2, 8, 256], arena + 24 * KB)
        match = sb("match", [P, 8, TOPK, TOPK], arena + 40 * KB)
        top_v = sb("top_v", [P, 2, PEER_ROWS, TOPK], arena + 48 * KB)
        top_i = sb("top_i", [P, 2, PEER_ROWS, TOPK], arena + 50 * KB, U32)
        top_f = sb("top_f", [P, 2, PEER_ROWS, TOPK], arena + 52 * KB)
        best_v = sb("best_v", [P, 2, 8, TOPK], arena + 54 * KB)
        best_i = sb("best_i", [P, 2, 8, TOPK], arena + 55 * KB, U32)
        half_i = sb("half_i", [P, 2, 2, P], arena + 56 * KB, U32)
        half_f = sb("half_f", [P, 2, 2, P], arena + 58 * KB)
        sel = sb("sel", [P, 2, 2, P], arena + 60 * KB)
        gate_tok = sb("gate_tok", [P, 2, P], arena + 62 * KB)
        gate_sum = sb("gate_sum", [P, 2, 2, 8], arena + 63 * KB)
        stage_raw = sb("stage_raw", [P, 2, 512], scratch)
        stage_sq = sb("stage_sq", [P, 2, 512], scratch + 4 * KB)
        stage_rs = sb("stage_rs", [P, 2, 512], scratch + 8 * KB)
        stage_y = sb("stage_y", [P, 2, 512], scratch + 12 * KB)
        ada_rows = sb("ada_rows", [4, 2, 512], scratch + 12 * KB)
        stage_z = sb("stage_z", [P, 2, 512], scratch + 16 * KB)
        consts = sb("consts", [P, 4, P], scratch + 20 * KB)
        ident, ones, ones_head, rot = (consts[:, n, :] for n in range(4))
        small = sb("small", [P, N_SMALL], scratch + 22 * KB)
        mod = sb("mod", [P, 2, ADA_CHUNKS, 2], scratch + 24 * KB + 512)
        cs = sb("cs", [P, KC, 2], scratch + 25 * KB + 768)
        cs_split = sb("cs_split", [P, KC, 4], scratch + 25 * KB + 832, F32R)
        tiny = sb("tiny", [P, 64], scratch + 26 * KB)
        mem = sb("mem", [P, KC, NT], scratch + 27 * KB)
        G = sb("G", [P, P, NT], gates_at)
        peer_at = gates_at + 128 * KB
        idx_T = sb("idx_T", [P, 3, NT], peer_at)
        iota = sb("iota", [P, P], peer_at + 3 * KB)
        spread1 = sb("spread1", [P, 4, TOKENS_PER_GROUP, P], peer_at + 4 * KB)
        spread2 = sb("spread2", [P, 4, TOKENS_PER_GROUP, P], peer_at + 8 * KB)
        gelu = sb("gelu", [P, R, NT], base + 56 * KB)
        gelu_in = sb("gelu_in", [P, R, NT], base + 60 * KB)
        pw = sb("pw", [P, 2, NT], peer_at + 2 * KB)
        pw_hi = sb("pw_hi", [P, 2, NT], peer_at + 4 * KB, F32R)
        pw_lo = sb("pw_lo", [P, 2, NT], peer_at + 6 * KB, F32R)
        zeros = sb("zeros", [P, 512], peer_at + 12 * KB)

        bank = [ctx.enter_context(nc.psum_tensor(f"bank{n}", [P, 512], F32)) for n in range(8)]

        in_loaded = sem("in_loaded")
        x_loaded = sem("x_loaded")
        rows_ready = sem("rows_ready")
        turned = sem("turned")
        mod_stored = sem("mod_stored")
        cs_ready = sem("cs_ready")
        mod_ready = sem("mod_ready")
        mem_split = sem("mem_split")
        raw_loaded = [sem(f"raw_loaded{s}") for s in range(R)]
        hi_ready = sem("hi_ready")
        lo_ready = sem("lo_ready")
        tile_used = sem("tile_used")
        x_done = sem("x_done")
        sq_ready = sem("sq_ready")
        sq_used = sem("sq_used")
        x_sq_ready = sem("x_sq_ready")
        x_sums_ready = sem("x_sums_ready")
        mem_sums = sem("mem_sums")
        mem_sq = sem("mem_sq")
        row_ready = sem("row_ready")
        fanned = sem("fanned")
        rs_ready = sem("rs_ready")
        mem_root = sem("mem_root")
        z_ready = sem("z_ready")
        y_ready = sem("y_ready")
        hh_ready = sem("hh_ready")
        hl_ready = sem("hl_ready")
        silu_done = sem("silu_done")
        a_ready = sem("a_ready")
        act_hi_ready = sem("act_hi_ready")
        act_lo_ready = sem("act_lo_ready")
        dve_chain = sem("dve_chain")
        act_chain = sem("act_chain")
        table_loaded = sem("table_loaded")
        const_made = sem("const_made")
        lam_ready = sem("lam_ready")
        out_stored = sem("out_stored")
        gelu_stored = [sem(f"gelu_stored{q}") for q in range(R)]
        gelu_loaded = [sem(f"gelu_loaded{q}") for q in range(R)]
        stage_sems = {}

        def of(stage, name):
            key = f"{stage}_{name}"
            if key not in stage_sems:
                stage_sems[key] = sem(key)
            return stage_sems[key]

        def sm(name, c=0, n=1):
            at = SMALL[name][0] + c
            return small[:, at:at + n]

        def h_ap(kind, c, halves):
            return H[:, :, kind, c, :] if halves == "LC" else H[:, "LC".index(halves), kind, c, :]

        def cols(buf, halves):
            return buf.rearrange("p (a n) -> p a n", a=2) if halves == "LC" else buf[:, 0:NT]

        def width(halves):
            return NT * len(halves)

        def mod_col(layer, which, c, half):
            return mod[:, layer, which * KC + c, half:half + 1]

        def x_src(halves):
            return lambda c: X[:, :, c, :] if halves == "LC" else X[:, 0, c, :]

        def modulated(layer, shift, scale):
            return (lambda c, half: mod_col(layer, scale, c, half)), (lambda c, half: mod_col(layer, shift, c, half))

        def gain(name, per_chunk=True):
            return (lambda c, half: sm(name, c if per_chunk else 0)), None

        whole = [(list(range(KC)), D)]
        NORMS = {}
        chunk_at = summed_at = own_at = shifted_at = group_at = 0
        for name, halves, groups, src, (scale, shift), summed in (
                ("pre0", "LC", whole, x_src("LC"), modulated(0, 0, 1), False),
                ("mix_a", "LC", whole, x_src("LC"), modulated(0, 3, 4), True),
                ("sub_a", "LC", [(list(range(KC)), P)], lambda c: Q[:, c, :].rearrange("p (a n) -> p a n", a=2),
                 gain("a_sub", False), False),
                ("post0", "LC", whole, x_src("LC"), modulated(0, 6, 7), True),
                ("pre1", "LC", whole, x_src("LC"), modulated(1, 0, 1), True),
                ("mix_b", "LC", whole, x_src("LC"), modulated(1, 3, 4), True),
                ("post1", "L", whole, x_src("L"), modulated(1, 6, 7), True),
                ("mix_c", "L", whole, x_src("L"), gain("g_mix"), True),
                ("og_c", "L", [([0, 1, 2], 3 * P), ([3, 4, 5], 3 * P), ([6, 7], 2 * P)], lambda c: Qc[:, c, :],
                 gain("og"), False),
                ("ffn_c", "L", whole, x_src("L"), gain("g_ffn"), True)):
            NORMS[name] = dict(halves=halves, groups=groups, src=src, scale=scale, shift=shift, summed=summed,
                               chunk_at=chunk_at, update=summed_at, own_at=own_at)
            chunk_at += KC
            summed_at += summed
            NORMS[name].update(shifted_at=shifted_at, group_at=group_at)
            group_at += len(groups)
            shifted_at += KC if shift else 0
            own_at += 0 if summed else KC

        def fan_bank(c):
            return bank[(1, 2, 3, 7)[c % 4]]

        def z_buf(c):
            return (stage_z if c % 4 < 2 else stage_raw)[:, c % 2, :]

        def sq_buf(q, i):
            return stage_sq[:, q, :] if q < 2 else stage_raw[:, 0, :] if q == 2 else stage_z[:, i, :]

        def norm_done(name):
            return NORMS[name]["chunk_at"] + KC

        def tile_list(*parts):
            got = []
            for kind, n, halves, gain_name, roped, to in parts:
                got += [dict(kind=kind, halves=halves, gain=gain_name, rope=roped, to=to, c=c) for c in range(n)]
            y = z = 0
            for t in got:
                t["y"] = y = y + (t["kind"] == "n")
                t["z"] = z = z + (t["kind"] != "n" or t["rope"])
            return got

        PROJ = {
            "qkv_a": tile_list(("n", 8, "LC", "a_q", True, "Q"), ("n", 8, "LC", "a_k", True, "K"),
                               ("v", 8, "LC", None, False, "V")),
            "qkv_b": tile_list(("n", 2, "LC", "b_k", True, "K2"), ("v", 2, "LC", None, False, "V"),
                               ("n", 8, "L", "b_q", True, "Q")),
            "proj_c": tile_list(("n", 2, "C", "mem_k", False, "K6"), ("v", 2, "C", None, False, "V6"),
                                ("n", 3, "L", "dil_q", False, "Q0"), ("n", 3, "L", "dil_k", False, "K0"),
                                ("v", 3, "L", None, False, "V0"), ("n", 3, "L", "moba_q", False, "Q3"),
                                ("n", 3, "L", "moba_k", False, "K3"), ("v", 3, "L", None, False, "V3"),
                                ("n", 2, "L", "mem_q", False, "Q6")),
            "peer_q": tile_list(("s", PEER_ROWS, "L", None, False, "S")),
        }

        PAIRS = {
            "pair_a": dict(proj="qkv_a", units=[(p, q) for p in range(KC) for q in range(4)], per=4),
            "pair_b": dict(proj="qkv_b", units=[(p, q) for p in range(KC) for q in range(2)], per=2),
            "pair_c": dict(proj="proj_c", units=[(p, q) for p in range(KC) for q in range(2)], per=2),
        }

        LAG = 2

        def ada_group(pair, u):
            part = {"pair_a": 1, "pair_b": 2}.get(pair)
            return None if part is None or not 0 <= u < len(PAIRS[pair]["units"]) else sum(ADA_PART[:part]) + u // 2

        def ada_after(pair, u, k):
            return ada_group(pair, u - k) if (u - k) % 2 == 1 else None

        def ada_splits(pair, u):
            part = {"pair_a": 1, "pair_b": 2}.get(pair)
            steps = len(PAIRS[pair]["units"])
            if part is None or u > steps:
                return []
            return [FIRST[f"ada{part}"] + n for n in range(max(2 * u + 2, AHEAD), min(2 * u + 4, 2 * steps + AHEAD))]

        def ada_half(u):
            return range(2 * (u % 2), 2 * (u % 2) + 2)

        def ada_first(g):
            part = 0 if g < ADA_PART[0] else 1 if g < ADA_PART[0] + ADA_PART[1] else 2
            return FIRST[f"ada{part}"] + ADA_TILES * (g - sum(ADA_PART[:part]))

        def ada_banks(g):
            if g < ADA_PART[0]:
                return bank[4 + g % 2], bank[6 + g % 2]
            return (bank[5], bank[7]) if g < ADA_PART[0] + ADA_PART[1] else (bank[7], bank[6])

        def value_bank(pair, p):
            return bank[6 + p % 2 if pair == "pair_c" else 6]

        def unit_keys(pair, q):
            if pair == "pair_a":
                return (0, 512) if q < 2 else (NT, 512)
            return (0, 512) if pair == "pair_b" else (0, NT)

        def proj_bank(k):
            return bank[(1, 6, 7)[k % 3]]

        block = ctx.enter_context(nc.Block())

        @block.sync
        def _(sp):
            for to, src in ((small[:, :], small_in), (consts[:, :, :], const_in)):
                sp.dma_start(to, src).then_inc(in_loaded, 16)

            def load_tile(i, s, first):
                if not first:
                    sp.wait_ge(lo_ready, R * i + s - R + 1)
                sp.dma_start(raw[:, s, :], w_stream[bass.ds(R * i + s, 1)].rearrange("o p n -> p (o n)")
                             ).then_inc(raw_loaded[s], 16)

            for s in range(R):
                load_tile(0, s, True)
            for to, src in ((mem[:, :, :], mem_in), (X[:, :, :, :], x_in)):
                sp.dma_start(to, src).then_inc(x_loaded, 16)
            with sp.Fori(1, N_TILES // R) as i:
                for s in range(R):
                    load_tile(i, s, False)
            for c in range(KC):
                sp.wait_ge(of("peer", "out_ready"), c + 1)
                sp.dma_start(out[:, c, :], X[:, 0, c, :]).then_inc(out_stored, 16)
            sp.wait_ge(out_stored, 16 * KC)

        @block.scalar
        def _(act):
            chain = [0]

            def link(ins):
                chain[0] += 1
                ins.then_inc(act_chain, 1)
                act.wait_ge(act_chain, chain[0])

            def split(t, i=0, per=0):
                if isinstance(i, int):
                    t, per = t + per * i, 0
                    if t >= N_TILES:
                        return
                s = t % R
                act.wait_ge(raw_loaded[s], 16 * (t // R + 1) + 16 * (per // R) * i)
                if t >= R or per:
                    act.wait_ge(tile_used, t - R + 1 + per * i)
                nc.scalar.activation(w_hi[:, s, :], raw[:, s, :], ACT.Copy).then_inc(hi_ready, 1)

            def ada_evac(g):
                act.wait_ge(tile_used, ada_first(g) + ADA_TILES)
                if g >= 2:
                    act.wait_ge(turned, g - 1)
                nc.scalar.activation(ada_rows[:, g % 2, :], ada_banks(g)[0][0:4, :], ACT.Copy).then_inc(rows_ready, 1)

            def norm(name):
                n = NORMS[name]
                hv = n["halves"]

                def high(c):
                    act.wait_ge(z_ready, n["chunk_at"] + c + 1)
                    if n["shift"] is None:
                        ins = nc.scalar.activation(h_ap(0, c, hv), cols(z_buf(c), hv), ACT.Copy)
                    else:
                        for b in range(len(hv)):
                            half = "LC".index(hv[b])
                            ins = nc.scalar.activation(H[:, half, 0, c, :], z_buf(c)[:, b * NT:(b + 1) * NT], ACT.Identity,
                                                       bias=n["shift"](c, half), scale=n["scale"](c, half))
                    ins.then_inc(hh_ready, 1)

                def root(g):
                    if g >= 2:
                        act.wait_ge(z_ready, n["chunk_at"] + n["groups"][g - 2][0][-1] + 1)
                    rows = slice(0, KC if name == "sub_a" else P)
                    nc.scalar.activation(stage_rs[rows, g % 2, 0:width(hv)], bank[g][rows, 0:width(hv)], ACT.Sqrt,
                                         bias=tiny[rows, 0:1]).then_inc(rs_ready, 1)

                link(nc.scalar.activation(tiny[:, 9:10], tiny[:, 0:1], ACT.Sqrt))
                if n["summed"]:
                    act.wait_ge(x_sums_ready, n["update"] + 1)
                    root(0)
                elif name == "pre0":
                    act.wait_ge(sq_used, KC)
                    root(0)
                else:
                    at = 0
                    for g, (chunks, size) in enumerate(n["groups"]):
                        for c in chunks:
                            act.wait_ge(of({"sub_a": "pair_a", "og_c": "pair_c"}[name], "o_ready"), c + 1)
                            act.wait_ge(sq_used, n["own_at"] + at - 1)
                            nc.scalar.activation(cols(stage_sq[:, at % 2, :], hv), n["src"](c), ACT.Square,
                                                 scale=size ** -0.5).then_inc(sq_ready, 1)
                            at += 1
                        if g >= 1:
                            act.wait_ge(sq_used, n["own_at"] + n["groups"][g - 1][0][-1] + 1)
                            root(g - 1)
                        if g >= 2:
                            for c in n["groups"][g - 2][0]:
                                high(c)
                    act.wait_ge(sq_used, n["own_at"] + KC)
                    root(len(n["groups"]) - 1)
                for chunks, _ in n["groups"][-2:]:
                    for c in chunks:
                        high(c)

            def squares(update, halves, i, q):
                act.wait_ge(x_done, KC * update + q + 1 + 4 * i)
                src = X[:, :, 4 * i + q, :] if halves == "LC" else X[:, 0, 4 * i + q, :]
                nc.scalar.activation(cols(sq_buf(q, i), halves), src, ACT.Square, scale=D ** -0.5
                                     ).then_inc(x_sq_ready, 1)

            def ffn(f, halves, update):
                w = width(halves)
                t0, t1 = FIRST[f"wi{f}"], FIRST[f"wo{f}"]
                link(nc.scalar.activation(tiny[:, 8:9], tiny[:, 0:1], ACT.Silu))

                def chunks(i):
                    for jj in range(2):
                        t = t0 + 2 * jj
                        split(t + AHEAD, i, 4)
                        act.wait_ge(tile_used, t + 1 + 4 * i)
                        nc.scalar.activation(stage_raw[:, jj, 0:w], bank[2 * jj][:, 0:w], ACT.Silu
                                             ).then_inc(silu_done, 1)
                        split(t + 1 + AHEAD, i, 4)
                        act.wait_ge(a_ready, FC * f + 2 * i + jj + 1)
                        nc.scalar.activation(act_hi[:, 2 * i + jj, 0:w], stage_y[:, jj, 0:w], ACT.Copy
                                             ).then_inc(act_hi_ready, 1)

                chunks(0)
                with act.Fori(1, FC // 2) as i:
                    chunks(i)
                with act.Fori(0, 2) as i:
                    for q in range(4):
                        for k in range(WO_T):
                            split(t1 + WO_T * q + k + AHEAD, i, 4 * WO_T)
                        squares(update, halves, i, q)

            def project(stage):
                tiles = PROJ[stage]
                t0 = FIRST[stage]

                def root(k):
                    if tiles[k]["kind"] != "n":
                        return
                    y, w = tiles[k]["y"], width(tiles[k]["halves"])
                    act.wait_ge(of(stage, "ss_ready"), y)
                    if y > 2:
                        act.wait_ge(of(stage, "y_ready"), y - 2)
                    nc.scalar.activation(stage_rs[:, y % 2, 0:w], bank[2 + y % 2][:, 0:w], ACT.Sqrt, bias=tiny[:, 0:1]
                                         ).then_inc(of(stage, "rs_ready"), 1)

                for k, t in enumerate(tiles):
                    w = width(t["halves"])
                    split(t0 + k + AHEAD)
                    act.wait_ge(tile_used, t0 + k + 1)
                    if k >= 2:
                        old = tiles[k - 2]
                        if old["kind"] == "n":
                            act.wait_ge(of(stage, "y_ready"), old["y"])
                        else:
                            act.wait_ge(of(stage, "rot_ready"), old["z"])
                    ins = nc.scalar.activation(stage_raw[:, k % 2, 0:w], proj_bank(k)[:, 0:w], ACT.Copy)
                    ins.then_inc(of(stage, "evac_ready"), 1)
                    if t["kind"] == "n":
                        y = t["y"]
                        if y > 2:
                            act.wait_ge(of(stage, "ss_ready"), y - 2)
                        nc.scalar.activation(stage_sq[:, y % 2, 0:w], proj_bank(k)[:, 0:w], ACT.Square,
                                             scale=HEAD ** -0.5).then_inc(of(stage, "sq_ready"), 1)
                    if k >= 1:
                        root(k - 1)
                root(len(tiles) - 1)

            def attend(pair):
                plan = PAIRS[pair]
                units, per = plan["units"], plan["per"]
                diff = pair == "pair_a"

                def exps(u):
                    p, q = units[u]
                    lo, hi = unit_keys(pair, q)
                    n = hi - lo
                    act.wait_ge(of(pair, "max_ready"), u + 1)
                    if u >= 3:
                        act.wait_ge(of(pair, "tr_ready"), u - 2)
                    for c in range(2):
                        src = bank[2 * (u % 2) + c][:, 0:n] if diff else logits[:, u % 2, c, 0:n]
                        ins = nc.scalar.activation(probs[:, u % 3, c, 0:n], src, ACT.Exp,
                                                   bias=tiny[:, 16 + 2 * (u % 2) + c:17 + 2 * (u % 2) + c],
                                                   scale=SCALE if diff else 1.0,
                                                   accum_out=tiny[:, 20 + 2 * (u % 3) + c:21 + 2 * (u % 3) + c])
                    if pair == "pair_b":
                        ins = nc.scalar.activation(tiny[:, 36 + 2 * (u % 3):38 + 2 * (u % 3)],
                                                   tiny[:, 28 + 2 * (u % 2):30 + 2 * (u % 2)], ACT.Exp)
                    ins.then_inc(of(pair, "p_ready"), 1)

                def copies(u):
                    p, q = units[u]
                    lo, hi = unit_keys(pair, q)
                    act.wait_ge(of(pair, "tr_ready"), u + 1)
                    if p >= 2:
                        act.wait_ge(of(pair, "pv_ready"), p - 1)
                    if diff:
                        to = pT[:, p % 2, :].rearrange("p (k q) -> p k q", k=4)[:, lo // P:hi // P, q * P:(q + 1) * P]
                        ins = nc.scalar.activation(to, bank[4][:, 0:hi - lo].rearrange("p (k q) -> p k q", q=P),
                                                   ACT.Copy)
                    else:
                        nk = hi // P
                        for c in range(2):
                            to = pT[:, p % 2, c * D:c * D + nk * NT].rearrange("p (k q) -> p k q", k=nk)[
                                :, :, q * P:(q + 1) * P]
                            ins = nc.scalar.activation(to, bank[4 + c][:, 0:hi].rearrange("p (k q) -> p k q", q=P),
                                                       ACT.Copy)
                    ins.then_inc(of(pair, "pT_ready"), 1)

                def o_out(p):
                    act.wait_ge(of(pair, "pv_ready"), p + 1)
                    if pair == "pair_b":
                        nc.scalar.activation(H[:, 0, 0, p, :], value_bank(pair, p)[:, 0:NT], ACT.Copy
                                             ).then_inc(of(pair, "o_ready"), 1)
                    elif pair == "pair_a":
                        nc.scalar.activation(Q[:, p, :], value_bank(pair, p)[:, :], ACT.Copy
                                             ).then_inc(of(pair, "o_ready"), 1)
                    else:
                        nc.scalar.activation(Qc[:, p, :], value_bank(pair, p)[:, 0:NT], ACT.Copy
                                             ).then_inc(of(pair, "o_ready"), 1)

                for u in range(len(units) + LAG + 1):
                    g = ada_after(pair, u, 1)
                    if g is not None:
                        ada_evac(g)
                    for t in ada_splits(pair, u):
                        split(t)
                    if LAG <= u < len(units) + LAG:
                        copies(u - LAG)
                    if u < len(units):
                        exps(u)
                    if u > LAG and (u - LAG) % per == 0:
                        o_out((u - LAG) // per - 1)

            def project_out(stage, halves, update):
                with act.Fori(0, 2) as i:
                    for q in range(4):
                        split(FIRST[stage] + q + AHEAD, i, 4)
                        squares(update, halves, i, q)

            act.wait_ge(in_loaded, 32)
            act.wait_ge(const_made, 1)
            nc.scalar.activation(cs[:, :, :], sm("c", 0, 2 * KC).rearrange("p (k v) -> p k v", v=2), ACT.Silu
                                 ).then_inc(cs_ready, 1)
            act.wait_ge(cs_ready, 1)
            nc.scalar.activation(cs_split[:, :, 0:2], cs[:, :, :], ACT.Copy).then_inc(cs_ready, 1)
            for t in range(AHEAD):
                split(t)
            act.wait_ge(lam_ready, 1)
            nc.scalar.activation(tiny[:, 4:6], tiny[:, 2:4], ACT.Exp).then_inc(lam_ready, 1)
            for g in range(ADA_PART[0]):
                for n in range(ADA_TILES):
                    split(ada_first(g) + n + AHEAD)
                if g >= 1:
                    ada_evac(g - 1)
                c = g - 2
                if c == 0:
                    act.wait_ge(x_loaded, 32)
                if 0 <= c < KC:
                    if c >= 2:
                        act.wait_ge(mem_sums, c - 1)
                        act.wait_ge(sq_used, c - 1)
                    nc.scalar.activation(stage_z[:, c % 2, 0:NT], mem[:, c, :], ACT.Square, scale=D ** -0.5
                                         ).then_inc(mem_sq, 1)
                    nc.scalar.activation(cols(stage_sq[:, c % 2, :], "LC"), X[:, :, c, :], ACT.Square, scale=D ** -0.5
                                         ).then_inc(sq_ready, 1)
            ada_evac(ADA_PART[0] - 1)
            act.wait_ge(mem_sums, KC)
            nc.scalar.activation(stage_rs[:, 1, 0:NT], bank[1][:, 0:NT], ACT.Sqrt, bias=tiny[:, 0:1]
                                 ).then_inc(mem_root, 1)
            norm("pre0")
            ffn(0, "LC", 0)
            act.wait_ge(x_done, KC)
            act.dma_start(rope[:, :, :], rope_in).then_inc(table_loaded, 16)
            act.dma_start(fan[:, :, :], fan_in).then_inc(table_loaded, 16)
            norm("mix_a")
            project("qkv_a")
            attend("pair_a")
            norm("sub_a")
            project_out("out_a", "LC", 1)
            norm("post0")
            ffn(1, "LC", 2)
            norm("pre1")
            ffn(2, "LC", 3)
            act.wait_ge(x_done, 4 * KC)
            act.dma_start(rope[:, :, :], rope_in).then_inc(table_loaded, 16)
            act.dma_start(mask[:, :, :], mask_in).then_inc(table_loaded, 16)
            norm("mix_b")
            project("qkv_b")
            attend("pair_b")
            project_out("out_b", "L", 4)
            norm("post1")
            nc.scalar.activation(H[:, 1, 0, :, :], mem[:, :, :], ACT.Copy).then_inc(mem_split, 1)
            ffn(3, "L", 5)
            act.wait_ge(x_done, 6 * KC)
            act.dma_start(bias[:, :, :, :], bias_in).then_inc(table_loaded, 16)
            norm("mix_c")
            act.wait_ge(hl_ready, norm_done("mix_c"))
            project("proj_c")
            attend("pair_c")
            norm("og_c")
            project_out("out_c", "L", 6)
            act.wait_ge(x_done, 7 * KC)
            act.dma_start(sub[:, :, :], sub_in).then_inc(table_loaded, 16)
            norm("ffn_c")
            project("peer_q")

            t0 = FIRST["peer"]
            t1, t2 = t0 + EARLY_CHUNKS, t0 + 2 * EARLY_CHUNKS

            def gelu_table():
                link(nc.scalar.activation(tiny_gelu, zeros[:, 0:1], ACT.Gelu))

            tiny_gelu = gelu_in[:, 0, 0:1]
            gelu_table()

            def early(i, q, first):
                c = R * i + q
                split(t0 + q + AHEAD, i, R)
                act.wait_ge(tile_used, t0 + q + 1 + R * i)
                if not first:
                    act.wait_ge(gelu_stored[q], 16 * i)
                nc.scalar.activation(gelu[:, q, :], bank[4 + q % 2][:, 0:NT], ACT.Gelu).then_inc(of("peer", "gelu"), 1)
                act.wait_ge(of("peer", "gelu"), c + 1)
                act.dma_start(gelu_dram[bass.ds(c, 1)].rearrange("o p n -> p (o n)"), gelu[:, q, :]
                              ).then_inc(gelu_stored[q], 16)

            for q in range(R):
                early(0, q, True)
            with act.Fori(1, EARLY_CHUNKS // R) as i:
                for q in range(R):
                    early(i, q, False)

            def load_gelu(i, q):
                act.dma_start(gelu_in[:, q, :], gelu_dram[bass.ds(R * i + q, 1)].rearrange("o p n -> p (o n)")
                              ).then_inc(gelu_loaded[q], 16)

            act.wait_ge(of("peer", "top_ready"), 1)
            nc.scalar.activation(best_v[:, :, :, :], best_v[:, :, :, :], ACT.Exp).then_inc(of("peer", "exp_ready"), 1)
            for q in range(R):
                act.wait_ge(gelu_stored[q], 16 * (EARLY_CHUNKS // R))
            for q in range(R):
                load_gelu(0, q)
            for n in range(3):
                act.wait_ge(of("peer", "idx_tr"), n + 1)
                nc.scalar.activation(idx_T[:, n, :], bank[n][:, 0:NT], ACT.Copy).then_inc(of("peer", "idx_ready"), 1)

            with act.Fori(0, NT // TOKENS_PER_GROUP // 4) as i:
                for b in range(4):
                    act.wait_ge(of("peer", "spread"), 4 * i + b + 1)
                    tok = TOKENS_PER_GROUP * (4 * i + b)
                    nc.scalar.activation(G[:, :, bass.ds(tok, TOKENS_PER_GROUP)],
                                         bank[4 + b][:, 0:TOKENS_PER_GROUP * P].rearrange("p (q e) -> p e q", q=TOKENS_PER_GROUP), ACT.Copy
                                         ).then_inc(of("peer", "gates"), 1)

            def hi_of(c, b):
                act.wait_ge(of("peer", "w_ready"), c + 1)
                nc.scalar.activation(pw_hi[:, b, :], pw[:, b, :], ACT.Copy).then_inc(of("peer", "w_hi"), 1)

            hi_of(0, 0)

            def early_v(i, q, last):
                if not (last and q == R - 1):
                    act.wait_ge(tile_used, t1 + q + R * i)
                    hi_of(R * i + q + 1, (q + 1) % 2)
                split(t1 + q + AHEAD, i, R)
                if not last:
                    load_gelu(i + 1, q)

            with act.Fori(0, EARLY_CHUNKS // R - 1) as i:
                for q in range(R):
                    early_v(i, q, False)
            for q in range(R):
                early_v(EARLY_CHUNKS // R - 1, q, True)

            gelu_table()

            def gelu_of(c, b):
                nc.scalar.activation(gelu[:, b, :], bank[4 + b][:, 0:NT], ACT.Gelu).then_inc(of("peer", "gelu"), 1)

            for b in range(2):
                split(t2 + b + AHEAD)
                act.wait_ge(tile_used, t2 + b + 1)
                gelu_of(EARLY_CHUNKS + b, b)
                hi_of(EARLY_CHUNKS + b, b)

            def two_chunks(i):
                for b in range(2):
                    t = t2 + 2 + 2 * b
                    c = EARLY_CHUNKS + 2 * i + 2 + b
                    split(t + AHEAD, i, 4)
                    act.wait_ge(tile_used, t + 1 + 4 * i)
                    gelu_of(c, b)
                    split(t + 1 + AHEAD, i, 4)
                    act.wait_ge(tile_used, t + 2 + 4 * i)
                    hi_of(c, b)

            with act.Fori(0, (EXPERT_CHUNKS - EARLY_CHUNKS) // 2 - 2) as i:
                two_chunks(i)
            two_chunks((EXPERT_CHUNKS - EARLY_CHUNKS) // 2 - 2)

        @block.vector
        def _(dve):
            chain = [0]

            def link(ins):
                chain[0] += 1
                ins.then_inc(dve_chain, 1)
                dve.wait_ge(dve_chain, chain[0])

            def split(t, i=0, per=0):
                if isinstance(i, int):
                    t, per = t + per * i, 0
                    if t >= N_TILES:
                        return
                s = t % R
                dve.wait_ge(hi_ready, t + 1 + per * i)
                nc.vector.tensor_tensor(w_lo[:, s, :], raw[:, s, :], w_hi[:, s, :].bitcast(F32), ALU.subtract
                                        ).then_inc(lo_ready, 1)

            def ada_store(g):
                dve.wait_ge(turned, g + 1)
                to = mod[:, :, :, :].rearrange("p l j v -> p (l j) v")[:, 4 * g:4 * g + 4, :]
                src = ada_banks(g)[1][:, 0:16].rearrange("p (j v) -> p j v", v=4)
                link(nc.vector.tensor_tensor(to, src[:, :, 0:2], sm("ada_b", 4 * g, 4)[:, :, None].to_broadcast([P, 4, 2]),
                                             ALU.add))
                nc.vector.tensor_tensor(to, to, src[:, :, 2:4], ALU.add).then_inc(mod_stored, 1)

            def norm(name):
                n = NORMS[name]
                hv = n["halves"]
                w = width(hv)

                def low(c):
                    dve.wait_ge(hh_ready, n["chunk_at"] + c + 1)
                    y = z_buf(c)
                    if n["shift"] is not None:
                        dve.wait_ge(y_ready, n["shifted_at"] + c + 1)
                        y = stage_y[:, c % 2, :]
                    nc.vector.tensor_tensor(h_ap(1, c, hv), cols(y, hv), h_ap(0, c, hv).bitcast(F32), ALU.subtract
                                            ).then_inc(hl_ready, 1)

                for g, (chunks, _) in enumerate(n["groups"]):
                    rs = stage_rs[:, g % 2, :]
                    dve.wait_ge(rs_ready, n["group_at"] + g + 1)
                    if name == "sub_a":
                        nc.vector.reciprocal(rs[0:KC, :], rs[0:KC, :]).then_inc(row_ready, 1)
                    else:
                        link(nc.vector.reciprocal(rs[:, 0:w], rs[:, 0:w]))
                    for c in chunks:
                        if name == "sub_a":
                            dve.wait_ge(fanned, c + 1)
                            rs = fan_bank(c)
                        if c >= 4:
                            dve.wait_ge(hl_ready, n["chunk_at"] + c - 3)
                        if n["shift"] is None:
                            ins = nc.vector.scalar_tensor_tensor(out=cols(z_buf(c), hv), in0=n["src"](c),
                                                                 scalar=n["scale"](c, 0), in1=cols(rs, hv),
                                                                 op0=ALU.mult, op1=ALU.mult)
                        else:
                            ins = nc.vector.tensor_tensor(cols(z_buf(c), hv), n["src"](c), cols(rs, hv), ALU.mult)
                        ins.then_inc(z_ready, 1)
                        if c >= 2:
                            low(c - 2)
                low(KC - 2)
                low(KC - 1)

            def update(m, half, src, gate):
                return nc.vector.scalar_tensor_tensor(out=X[:, half, m, :], in0=src, scalar=gate, in1=X[:, half, m, :],
                                                      op0=ALU.mult, op1=ALU.add)

            def ffn(f, layer, which, halves):
                w = width(halves)
                t0, t1 = FIRST[f"wi{f}"], FIRST[f"wo{f}"]

                def chunks(i):
                    for jj in range(2):
                        t = t0 + 2 * jj
                        j = FC * f + 2 * i + jj
                        split(t + AHEAD, i, 4)
                        split(t + 1 + AHEAD, i, 4)
                        dve.wait_ge(silu_done, j + 1)
                        dve.wait_ge(tile_used, t + 2 + 4 * i)
                        nc.vector.tensor_tensor(stage_y[:, jj, 0:w], stage_raw[:, jj, 0:w], bank[2 * jj + 1][:, 0:w],
                                                ALU.mult).then_inc(a_ready, 1)
                        dve.wait_ge(act_hi_ready, j + 1)
                        nc.vector.tensor_tensor(act_lo[:, 2 * i + jj, 0:w], stage_y[:, jj, 0:w],
                                                act_hi[:, 2 * i + jj, 0:w].bitcast(F32), ALU.subtract
                                                ).then_inc(act_lo_ready, 1)

                with dve.Fori(0, FC // 2) as i:
                    chunks(i)
                with dve.Fori(0, 2) as i:
                    for q in range(4):
                        m = 4 * i + q
                        for k in range(WO_T):
                            split(t1 + WO_T * q + k + AHEAD, i, 4 * WO_T)
                        dve.wait_ge(tile_used, t1 + WO_T * (q + 1) + 4 * WO_T * i)
                        for half in range(len(halves)):
                            ins = update(m, half, bank[4 + q][:, half * NT:(half + 1) * NT],
                                         mod[:, layer, bass.ds(which * KC + m, 1), half])
                        ins.then_inc(x_done, 1)

            def project(stage):
                tiles = PROJ[stage]
                t0 = FIRST[stage]

                def dest(t):
                    to, c, w = t["to"], t["c"], width(t["halves"])
                    if stage == "proj_c":
                        c += int(to[1])
                        return Qc[:, c, :] if to[0] == "Q" else Kc[:, c, :]
                    return (Q if to == "Q" else K)[:, c, 0:w]

                def scaled(k):
                    t = tiles[k]
                    if t["kind"] != "n":
                        return
                    y, w = t["y"], width(t["halves"])
                    rs = stage_rs[:, y % 2, 0:w]
                    dve.wait_ge(of(stage, "rs_ready"), y)
                    link(nc.vector.reciprocal(rs, rs))
                    to = stage_y[:, y % 2, 0:w] if t["rope"] else dest(t)
                    nc.vector.scalar_tensor_tensor(out=to, in0=stage_raw[:, k % 2, 0:w], scalar=sm(t["gain"]), in1=rs,
                                                   op0=ALU.mult, op1=ALU.mult).then_inc(of(stage, "y_ready"), 1)

                def second(k):
                    t = tiles[k]
                    w = width(t["halves"])
                    if t["kind"] == "n" and not t["rope"]:
                        return
                    y, z = t["y"], t["z"]
                    dve.wait_ge(of(stage, "rot_ready"), z)
                    src = bank[4 + z % 2][:, 0:w]
                    if t["kind"] == "v":
                        c = t["c"] + (int(t["to"][1]) if stage == "proj_c" else 0)
                        to = (Vc if stage == "proj_c" else V)[:, 0:w // P, c * P:(c + 1) * P]
                        ins = nc.vector.tensor_copy(to, src.rearrange("p (k e) -> p k e", e=P))
                    elif t["kind"] == "s":
                        ins = nc.vector.tensor_copy(S[:, :, t["c"], :], src.rearrange("p (k e) -> p k e", e=P))
                    else:
                        if z > 1:
                            dve.wait_ge(of(stage, "z_ready"), z - 1)
                        link(nc.vector.tensor_tensor(stage_z[:, 0, 0:w], src, rope[:, 1, 0:w], ALU.mult))
                        dve.wait_ge(of(stage, "cos_ready"), y)
                        if t["to"] == "K2":
                            link(nc.vector.tensor_tensor(stage_z[:, 0, 0:w], stage_z[:, 0, 0:w], stage_z[:, 1, 0:w],
                                                         ALU.add))
                            for kv in range(2):
                                for side in range(2):
                                    ins = nc.vector.tensor_copy(
                                        K[HEAD * side:HEAD * (side + 1), 2 * t["c"] + kv, 0:w],
                                        stage_z[HEAD * kv:HEAD * (kv + 1), 0, 0:w])
                        else:
                            ins = nc.vector.tensor_tensor(dest(t), stage_z[:, 0, 0:w], stage_z[:, 1, 0:w], ALU.add)
                    ins.then_inc(of(stage, "z_ready"), 1)

                for k in range(len(tiles) + 2):
                    if k < len(tiles):
                        split(t0 + k + AHEAD)
                    if 1 <= k <= len(tiles):
                        scaled(k - 1)
                    if k >= 2:
                        second(k - 2)

            def attend(pair):
                plan = PAIRS[pair]
                units, per = plan["units"], plan["per"]
                diff = pair == "pair_a"

                def maxima(u):
                    p, q = units[u]
                    lo, hi = unit_keys(pair, q)
                    n = hi - lo
                    b = u % 2
                    top = tiny[:, 32 + 2 * b:34 + 2 * b]
                    dve.wait_ge(of(pair, "s_ready"), u + 1)
                    if u >= 2:
                        dve.wait_ge(of(pair, "p_ready"), u - 1)
                    for c in range(2):
                        src = bank[2 * b + c][:, 0:n]
                        if diff:
                            ins = nc.vector.tensor_reduce(top[:, c:c + 1], src, AX_X, ALU.max)
                        else:
                            head = 2 * p + c
                            if pair == "pair_b":
                                add, least = mask[:, q, :], sm("sink", head)
                            else:
                                add = bias[:, head, q, :] if head < 12 else zeros[:, 0:NT]
                                least = -3.0e38
                            ins = nc.vector.tensor_tensor_reduce(logits[:, b, c, 0:n], src, add, SCALE, least,
                                                                 ALU.add, ALU.max, top[:, c:c + 1])
                    link(ins)
                    if pair == "pair_b":
                        nc.vector.tensor_tensor(tiny[:, 28 + 2 * b:30 + 2 * b], sm("sink", 2 * p, 2), top, ALU.subtract)
                    nc.vector.tensor_scalar(tiny[:, 16 + 2 * b:18 + 2 * b], top, -SCALE if diff else -1.0, None,
                                            ALU.mult).then_inc(of(pair, "max_ready"), 1)

                def weigh(u):
                    p, q = units[u]
                    lo, hi = unit_keys(pair, q)
                    n = hi - lo
                    r = u % 3
                    den = tiny[:, 20 + 2 * r:22 + 2 * r]
                    dve.wait_ge(of(pair, "p_ready"), u + 1)
                    if pair == "pair_b":
                        link(nc.vector.tensor_tensor(den, den, tiny[:, 36 + 2 * r:38 + 2 * r], ALU.add))
                    link(nc.vector.reciprocal(den, den))
                    if diff:
                        link(nc.vector.tensor_tensor(den[:, 1:2], den[:, 1:2], tiny[:, 6:7], ALU.mult))
                        link(nc.vector.tensor_scalar(probs[:, r, 0, 0:n], probs[:, r, 0, 0:n], den[:, 0:1], None,
                                                     ALU.mult))
                        ins = nc.vector.scalar_tensor_tensor(out=probs[:, r, 0, 0:n], in0=probs[:, r, 1, 0:n],
                                                             scalar=den[:, 1:2], in1=probs[:, r, 0, 0:n],
                                                             op0=ALU.mult, op1=ALU.add)
                    else:
                        for c in range(2):
                            ins = nc.vector.tensor_scalar(probs[:, r, c, 0:n], probs[:, r, c, 0:n], den[:, c:c + 1],
                                                          None, ALU.mult)
                    ins.then_inc(of(pair, "w_ready"), 1)

                def low(p):
                    dve.wait_ge(of(pair, "o_ready"), p + 1)
                    nc.vector.tensor_tensor(H[:, 0, 1, p, :], value_bank(pair, p)[:, 0:NT], H[:, 0, 0, p, :].bitcast(F32),
                                            ALU.subtract).then_inc(of(pair, "ol_ready"), 1)

                if diff:
                    dve.wait_ge(lam_ready, 2)
                    link(nc.vector.tensor_tensor(tiny[:, 6:7], tiny[:, 5:6], tiny[:, 4:5], ALU.subtract))
                    link(nc.vector.tensor_scalar(tiny[:, 6:7], tiny[:, 6:7], -LAM_INIT, None, ALU.add))
                if not diff:
                    dve.wait_ge(table_loaded, {"pair_b": 64, "pair_c": 80}[pair])
                for u in range(len(units) + LAG + 2):
                    g = ada_after(pair, u, 3)
                    if g is not None:
                        ada_store(g)
                    if u < len(units):
                        maxima(u)
                    if 1 <= u <= len(units):
                        weigh(u - 1)
                    if pair == "pair_b" and u > LAG + 1 and (u - LAG - 1) % per == 0:
                        low((u - LAG - 1) // per - 1)
                    if ada_after(pair, u, 1) is not None:
                        t = ada_first(ada_after(pair, u, 1)) + ADA_TILES - 1 + AHEAD
                        dve.wait_ge(lo_ready, t)
                        split(t)

            def project_out(stage, gate, halves):
                with dve.Fori(0, 2) as i:
                    for q in range(4):
                        m = 4 * i + q
                        split(FIRST[stage] + q + AHEAD, i, 4)
                        dve.wait_ge(tile_used, FIRST[stage] + q + 1 + 4 * i)
                        for half in range(len(halves)):
                            scalar = sm("one") if gate is None else mod[:, gate, bass.ds(5 * KC + m, 1), half]
                            ins = update(m, half, bank[4 + q][:, half * NT:(half + 1) * NT], scalar)
                        ins.then_inc(x_done, 1)

            nc.vector.memset(zeros[:, :], 0.0)
            link(nc.vector.memset(tiny[:, :], 0.0))
            nc.vector.memset(tiny[:, 0:1], EPS).then_inc(const_made, 1)
            dve.wait_ge(in_loaded, 32)
            lam = sm("lam", 0, 4 * HEAD).rearrange("p (a d) -> p a d", a=4)
            for n in range(2):
                ins = nc.vector.tensor_tensor_reduce(stage_z[:, n, 0:HEAD], lam[:, 2 * n, :], lam[:, 2 * n + 1, :],
                                                     1.0, 0.0, ALU.mult, ALU.add, tiny[:, 2 + n:3 + n])
            ins.then_inc(lam_ready, 1)
            link(nc.vector.tensor_scalar(sm("a_sub"), sm("a_sub"), 1.0 - LAM_INIT, None, ALU.mult))
            dve.wait_ge(cs_ready, 2)
            nc.vector.tensor_tensor(cs_split[:, :, 2:4], cs[:, :, :], cs_split[:, :, 0:2].bitcast(F32), ALU.subtract
                                    ).then_inc(cs_ready, 1)
            for t in range(AHEAD):
                split(t)
            for g in range(ADA_PART[0]):
                for n in range(ADA_TILES):
                    split(ada_first(g) + n + AHEAD)
                if g >= 1:
                    ada_store(g - 1)
            ada_store(ADA_PART[0] - 1)

            def adjust(layer, ones_more, halved):
                for which in ones_more:
                    part = mod[:, layer, which * KC:(which + 1) * KC, :]
                    ins = nc.vector.tensor_scalar(part, part, 1.0, None, ALU.add)
                for which in halved:
                    part = mod[:, layer, which * KC:(which + 1) * KC, :]
                    ins = nc.vector.tensor_scalar(part, part, 0.5, None, ALU.mult)
                return ins

            dve.wait_ge(mod_stored, ADA_PART[0])
            adjust(0, (1, 4), (2,)).then_inc(mod_ready, 1)
            dve.wait_ge(mod_ready, 1)

            norm("pre0")
            dve.wait_ge(mem_root, 1)
            link(nc.vector.reciprocal(stage_rs[:, 1, 0:NT], stage_rs[:, 1, 0:NT]))
            for c in range(KC):
                ins = nc.vector.scalar_tensor_tensor(out=mem[:, c, :], in0=mem[:, c, :], scalar=sm("g_mem", c),
                                                     in1=stage_rs[:, 1, 0:NT], op0=ALU.mult, op1=ALU.mult)
            ins.then_inc(mem_split, 1)
            ffn(0, 0, 2, "LC")
            norm("mix_a")
            dve.wait_ge(table_loaded, 32)
            project("qkv_a")
            attend("pair_a")
            dve.wait_ge(mod_stored, ADA_PART[0] + ADA_PART[1])
            adjust(0, (7,), (8,))
            adjust(1, (1, 4), (2,)).then_inc(mod_ready, 1)
            dve.wait_ge(mod_ready, 2)
            dve.wait_ge(of("pair_a", "o_ready"), KC)
            norm("sub_a")
            dve.wait_ge(lo_ready, FIRST["out_a"] + AHEAD)
            project_out("out_a", 0, "LC")
            norm("post0")
            ffn(1, 0, 8, "LC")
            norm("pre1")
            ffn(2, 1, 2, "LC")
            norm("mix_b")
            dve.wait_ge(table_loaded, 64)
            project("qkv_b")
            attend("pair_b")
            dve.wait_ge(mod_stored, sum(ADA_PART))
            adjust(1, (7,), (8,)).then_inc(mod_ready, 1)
            dve.wait_ge(mod_ready, 3)
            dve.wait_ge(lo_ready, FIRST["out_b"] + AHEAD)
            project_out("out_b", 1, "L")
            norm("post1")
            dve.wait_ge(mem_split, 2)
            nc.vector.tensor_tensor(H[:, 1, 1, :, :], mem[:, :, :], H[:, 1, 0, :, :].bitcast(F32), ALU.subtract
                                    ).then_inc(mem_split, 1)
            ffn(3, 1, 8, "L")
            norm("mix_c")
            project("proj_c")
            attend("pair_c")
            dve.wait_ge(of("pair_c", "o_ready"), KC)
            norm("og_c")
            project_out("out_c", None, "L")
            norm("ffn_c")
            project("peer_q")

            def best16(rows):
                def each(op):
                    for row in rows:
                        ins = op(*row)
                    link(ins)
                each(lambda s, v, ix: nc.vector.max(v[:, 0:8], s))
                each(lambda s, v, ix: nc.vector.max_index(ix[:, 0:8], v[:, 0:8], s))
                each(lambda s, v, ix: nc.vector.match_replace(s, v[:, 0:8], s, -3.0e38))
                each(lambda s, v, ix: nc.vector.max(v[:, 8:16], s))
                each(lambda s, v, ix: nc.vector.max_index(ix[:, 8:16], v[:, 8:16], s))

            dve.wait_ge(of("peer_q", "z_ready"), PEER_ROWS)
            best16([(S[:, t, r, :], top_v[:, t, r, :], top_i[:, t, r, :]) for t in range(2) for r in range(PEER_ROWS)])
            link(nc.vector.tensor_copy(top_f[:, :, :, :], top_i[:, :, :, :]))
            for t in range(2):
                pair = top_v[:, t, :, :].rearrange("p (h a) k -> p h a k", a=2)
                for h in range(8):
                    ins = nc.vector.tensor_tensor(
                        cand[:, t, h, :].rearrange("p (a b) -> p a b", a=TOPK),
                        pair[:, h, 0, :][:, :, None].to_broadcast([P, TOPK, TOPK]),
                        pair[:, h, 1, :][:, None, :].to_broadcast([P, TOPK, TOPK]), ALU.add)
            link(ins)
            best16([(cand[:, t, h, :], best_v[:, t, h, :], best_i[:, t, h, :]) for t in range(2) for h in range(8)])
            for t in range(2):
                flat_i = best_i[:, t, :, :].rearrange("p h k -> p (h k)")
                nc.vector.tensor_scalar(half_i[:, t, 0, :], flat_i, 4, None, ALU.logical_shift_right)
                ins = nc.vector.tensor_scalar(half_i[:, t, 1, :], flat_i, 15, None, ALU.bitwise_and)
            link(ins)
            link(nc.vector.tensor_copy(half_f[:, :, :, :], half_i[:, :, :, :]))
            for t in range(2):
                ins = nc.vector.tensor_tensor(gate_tok[:, t, :].rearrange("p (h k) -> p h k", k=TOPK),
                                              best_v[:, t, :, :], best_v[:, t, :, 0:1].to_broadcast([P, 8, TOPK]),
                                              ALU.subtract)
            link(ins)
            nc.vector.tensor_copy(best_v[:, :, :, :].rearrange("p t h k -> p t (h k)"), gate_tok[:, :, :]
                                  ).then_inc(of("peer", "top_ready"), 1)
            count = iota[:, 0:TOPK]
            dve.wait_ge(of("peer", "iota_ready"), 1)
            for t in range(2):
                for a in range(2):
                    link(nc.vector.tensor_tensor(
                        match[:, :, :, :],
                        half_f[:, t, a, :].rearrange("p (h k) -> p h k", k=TOPK)[:, :, :, None].to_broadcast(
                            [P, 8, TOPK, TOPK]),
                        count[:, None, None, :].to_broadcast([P, 8, TOPK, TOPK]), ALU.is_equal))
                    keys = top_f[:, t, :, :].rearrange("p (h a) j -> p h a j", a=2)[:, :, a, :]
                    link(nc.vector.tensor_tensor(match[:, :, :, :], match[:, :, :, :],
                                                 keys[:, :, None, :].to_broadcast([P, 8, TOPK, TOPK]), ALU.mult))
                    ins = nc.vector.tensor_reduce(sel[:, a, t, :].rearrange("p (h k) -> p h k", k=TOPK),
                                                  match[:, :, :, :], AX_X, ALU.add)
                    link(ins)
            dve.wait_ge(of("peer", "exp_ready"), 1)
            for t in range(2):
                ins = nc.vector.tensor_reduce(gate_sum[:, 0, t, :], best_v[:, t, :, :], AX_X, ALU.add)
            link(ins)
            link(nc.vector.reciprocal(gate_sum[:, 1, :, :], gate_sum[:, 0, :, :]))
            for t in range(2):
                ins = nc.vector.tensor_tensor(gate_tok[:, t, :].rearrange("p (h k) -> p h k", k=TOPK),
                                              best_v[:, t, :, :],
                                              gate_sum[:, 1, t, :][:, :, None].to_broadcast([P, 8, TOPK]), ALU.mult)
            ins.then_inc(of("peer", "routed"), 1)

            dve.wait_ge(of("peer", "idx_ready"), 3)

            def spread(i, b, first):
                if not first:
                    dve.wait_ge(of("peer", "spread"), 4 * i + b - 3)
                tok = TOKENS_PER_GROUP * (4 * i + b)
                shape = [P, TOKENS_PER_GROUP, P]
                for n, to in enumerate((spread1, spread2)):
                    keys = idx_T[:, n, bass.ds(tok, TOKENS_PER_GROUP)][:, :, None].to_broadcast(shape)
                    ins = nc.vector.tensor_tensor(to[:, b, :, :], iota[:, None, :].to_broadcast(shape), keys, ALU.is_equal)
                ins.then_inc(of("peer", "onehot"), 1)

            for b in range(4):
                spread(0, b, True)
            with dve.Fori(1, NT // TOKENS_PER_GROUP // 4) as i:
                for b in range(4):
                    spread(i, b, False)

            t0 = FIRST["peer"]
            t1, t2 = t0 + EARLY_CHUNKS, t0 + 2 * EARLY_CHUNKS

            def weight(c, b, src):
                nc.vector.tensor_tensor(pw[:, b, :], src, G[:, c, :], ALU.mult).then_inc(of("peer", "w_ready"), 1)

            def weight_low(c, b):
                dve.wait_ge(of("peer", "w_hi"), c + 1)
                nc.vector.tensor_tensor(pw_lo[:, b, :], pw[:, b, :], pw_hi[:, b, :].bitcast(F32), ALU.subtract
                                        ).then_inc(of("peer", "w_lo"), 1)

            def early_weight(i, q):
                dve.wait_ge(gelu_loaded[q], 16 * i + 16)
                weight(R * i + q, q % 2, gelu_in[:, q, :])

            dve.wait_ge(lo_ready, t1 + AHEAD)
            dve.wait_ge(of("peer", "gates"), NT // TOKENS_PER_GROUP)
            early_weight(0, 0)
            weight_low(0, 0)
            early_weight(0, 1)

            def early_v(i, last):
                for q in range(R):
                    if not (last and q + 1 >= R):
                        weight_low(R * i + q + 1, (q + 1) % 2)
                    if not (last and q + 2 >= R):
                        early_weight(i + (q + 2) // R, (q + 2) % R)
                    split(t1 + q + AHEAD, i, R)

            with dve.Fori(0, EARLY_CHUNKS // R - 1) as i:
                early_v(i, False)
            early_v(EARLY_CHUNKS // R - 1, True)

            def late_weight(c, b):
                dve.wait_ge(of("peer", "gelu"), c + 1)
                weight(c, b, gelu[:, b, :])
                weight_low(c, b)

            for b in range(2):
                split(t2 + b + AHEAD)
                late_weight(EARLY_CHUNKS + b, b)

            def two_chunks(i):
                for b in range(2):
                    t = t2 + 2 + 2 * b
                    split(t + AHEAD, i, 4)
                    split(t + 1 + AHEAD, i, 4)
                    late_weight(EARLY_CHUNKS + 2 * i + 2 + b, b)

            with dve.Fori(0, (EXPERT_CHUNKS - EARLY_CHUNKS) // 2 - 2) as i:
                two_chunks(i)
            two_chunks((EXPERT_CHUNKS - EARLY_CHUNKS) // 2 - 2)
            dve.wait_ge(tile_used, N_TILES)
            for c in range(KC):
                nc.vector.tensor_tensor(X[:, 0, c, :], X[:, 0, c, :], bank[c // 2][:, (c % 2) * NT:(c % 2 + 1) * NT],
                                        ALU.add).then_inc(of("peer", "out_ready"), 1)

        @block.gpsimd
        def _(pool):
            def norm(name):
                n = NORMS[name]
                for c in range(KC):
                    pool.wait_ge(z_ready, n["chunk_at"] + c + 1)
                    if c >= 2:
                        pool.wait_ge(hl_ready, n["chunk_at"] + c - 1)
                    for b in range(len(n["halves"])):
                        half = "LC".index(n["halves"][b])
                        cut = slice(b * NT, (b + 1) * NT)
                        ins = nc.gpsimd.tensor_scalar(stage_y[:, c % 2, cut], z_buf(c)[:, cut], n["scale"](c, half),
                                                      n["shift"](c, half), ALU.mult, ALU.add)
                    ins.then_inc(y_ready, 1)

            def project(stage):
                for t in PROJ[stage]:
                    if not t["rope"]:
                        continue
                    y, w = t["y"], width(t["halves"])
                    pool.wait_ge(of(stage, "y_ready"), y)
                    if t["z"] > 1:
                        pool.wait_ge(of(stage, "z_ready"), t["z"] - 1)
                    nc.gpsimd.tensor_tensor(stage_z[:, 1, 0:w], stage_y[:, y % 2, 0:w], rope[:, 0, 0:w], ALU.mult
                                            ).then_inc(of(stage, "cos_ready"), 1)

            def low_parts(first, n, mine):
                with pool.Fori(0, n // R) as i:
                    for q in mine:
                        t = first + AHEAD + q
                        if q == 0 and len(mine) < R:
                            pool.wait_ge(lo_ready, t + R * i)
                        pool.wait_ge(hi_ready, t + 1 + R * i)
                        nc.gpsimd.tensor_tensor(w_lo[:, t % R, :], raw[:, t % R, :], w_hi[:, t % R, :].bitcast(F32),
                                                ALU.subtract).then_inc(lo_ready, 1)

            for name in ("pre0", "mix_a", "qkv_a", "ada1", "post0", "pre1", "mix_b", "qkv_b", "ada2", "post1"):
                if name == "qkv_a":
                    pool.wait_ge(table_loaded, 32)
                if name == "qkv_b":
                    pool.wait_ge(table_loaded, 64)
                if name in PROJ:
                    project(name)
                elif name in NORMS:
                    norm(name)
                else:
                    low_parts(FIRST[name], ADA_TILES * ADA_PART[int(name[3:])], range(R - 1))
            pool.wait_ge(of("peer_q", "z_ready"), PEER_ROWS)
            nc.gpsimd.iota(iota[:, :], [[1, P]], base=0, channel_multiplier=0, allow_small_or_imprecise_dtypes=True
                           ).then_inc(of("peer", "iota_ready"), 1)
            low_parts(FIRST["peer"], EARLY_CHUNKS, range(R))

            pool.wait_ge(of("peer", "idx_ready"), 3)

            def spread(i, b, first):
                pool.wait_ge(of("peer", "onehot"), 4 * i + b + 1)
                tok = TOKENS_PER_GROUP * (4 * i + b)
                nc.gpsimd.tensor_tensor(
                    spread1[:, b, :, :], spread1[:, b, :, :],
                    idx_T[:, 2, bass.ds(tok, TOKENS_PER_GROUP)][:, :, None].to_broadcast([P, TOKENS_PER_GROUP, P]),
                    ALU.mult).then_inc(of("peer", "gated"), 1)

            for b in range(4):
                spread(0, b, True)
            with pool.Fori(1, NT // TOKENS_PER_GROUP // 4) as i:
                for b in range(4):
                    spread(i, b, False)

        @block.tensor
        def _(pe):
            def passes(to, s, block_at, hi, lo, first, last):
                cut = slice(block_at * P, (block_at + 1) * P)
                nc.tensor.matmul(to, w_hi[:, s, cut], hi, start=first, stop=False, skip_group_check=True)
                nc.tensor.matmul(to, w_hi[:, s, cut], lo, start=False, stop=False, skip_group_check=True)
                return nc.tensor.matmul(to, w_lo[:, s, cut], hi, start=False, stop=last, skip_group_check=True)

            def product(to, t, halves, i=0, per=0):
                pe.wait_ge(lo_ready, t + 1 + per * i)
                for k in range(KC):
                    ins = passes(to[:, 0:width(halves)], t % R, k, h_ap(0, k, halves), h_ap(1, k, halves),
                                 k == 0, k == KC - 1)
                ins.then_inc(tile_used, 1)

            def ada_product(g, tiles=range(ADA_TILES)):
                to = ada_banks(g)[0][0:4, :]
                if g < ADA_PART[0] and g >= 2:
                    pe.wait_ge(rows_ready, g - 1)
                elif g >= ADA_PART[0] and 0 in tiles:
                    pe.wait_ge(rows_ready, g)
                for n in tiles:
                    t = ada_first(g) + n
                    pe.wait_ge(lo_ready, t + 1)
                    for k in range(2):
                        for part in (w_hi, w_lo):
                            ins = nc.tensor.matmul(to, cs_split[:, 2 * n + k, :], part[:, t % R, k * 512:(k + 1) * 512],
                                                   start=n + k == 0 and part is w_hi,
                                                   stop=n == ADA_TILES - 1 and k == 1 and part is w_lo,
                                                   skip_group_check=True)
                    ins.then_inc(tile_used, 1)

            def ada_turn(g):
                pe.wait_ge(rows_ready, g + 1)
                if g >= 2:
                    pe.wait_ge(mod_stored, g - 1 if g < ADA_PART[0] else g)
                for j in range(4):
                    ins = nc.tensor.transpose(ada_banks(g)[1][:, 4 * j:4 * j + 4], ada_rows[:, g % 2, j * P:(j + 1) * P],
                                              ident[0:4, 0:4])
                ins.then_inc(turned, 1)

            def sums(name):
                n = NORMS[name]
                w = width(n["halves"])
                at = n["own_at"]
                for g, (chunks, _) in enumerate(n["groups"]):
                    for c in chunks:
                        pe.wait_ge(sq_ready, at + 1)
                        to, column = (bank[g][0:KC, 0:w], sm("pick", KC - 1 - c, KC)) if name == "sub_a" else (
                            bank[g][:, 0:w], ones)
                        ins = nc.tensor.matmul(to, column, stage_sq[:, (at - n["own_at"]) % 2, 0:w],
                                               start=c == chunks[0], stop=c == chunks[-1])
                        ins.then_inc(sq_used, 1)
                        at += 1

            def open_x_sums():
                nc.tensor.matmul(bank[0][:, :], zeros[:, 0:P], zeros[:, :], start=True, stop=False, skip_group_check=True)

            def x_sum(update, halves, i, q, last=False):
                w = width(halves)
                pe.wait_ge(x_sq_ready, KC * update + q + 1 + 4 * i)
                return nc.tensor.matmul(bank[0][:, 0:w], ones, sq_buf(q, i)[:, 0:w], start=False, stop=last,
                                        skip_group_check=True)

            def close_x_sums(update, halves):
                x_sum(update, halves, 0, 3)
                x_sum(update, halves, 1, 3, True).then_inc(x_sums_ready, 1)

            def fan_out(c):
                nc.tensor.matmul(fan_bank(c)[:, :], fan[:, c, :], stage_rs[0:KC, 0, :], start=True, stop=True
                                 ).then_inc(fanned, 1)

            def first_products(name, targets, t0, halves):
                pe.wait_ge(lo_ready, t0 + len(targets))
                w = width(halves)
                if name == "sub_a":
                    pe.wait_ge(row_ready, 1)
                    for c in range(4):
                        fan_out(c)
                for k in range(KC):
                    if name == "sub_a" and k + 4 < KC:
                        pe.wait_ge(z_ready, NORMS[name]["chunk_at"] + k + 1)
                        fan_out(k + 4)
                    pe.wait_ge(hl_ready, NORMS[name]["chunk_at"] + k + 1)
                    for n, to in enumerate(targets):
                        ins = passes(to[:, 0:w], (t0 + n) % R, k, h_ap(0, k, halves), h_ap(1, k, halves), k == 0,
                                     k == KC - 1)
                        if k == KC - 1:
                            ins.then_inc(tile_used, 1)

            def ffn(f, name, halves, update):
                w = width(halves)
                t0, t1 = FIRST[f"wi{f}"], FIRST[f"wo{f}"]
                first_products(name, bank[0:AHEAD], t0, halves)
                product(bank[AHEAD], t0 + AHEAD, halves)
                with pe.Fori(1, FC // 2) as i:
                    for q in range(4):
                        product(bank[q], t0 + q, halves, i, 4)
                pe.wait_ge(a_ready, FC * f + FC - 1)
                open_x_sums()
                with pe.Fori(0, 2) as i:
                    for q in range(4):
                        for kk in range(WO_T):
                            t = t1 + WO_T * q + kk
                            pe.wait_ge(lo_ready, t + 1 + 4 * WO_T * i)
                            pe.wait_ge(act_lo_ready, FC * f + min(FC, KC * (kk + 1)))
                            for k in range(min(KC, FC - KC * kk)):
                                j = KC * kk + k
                                ins = passes(bank[4 + q][:, 0:w], t % R, k, act_hi[:, j, 0:w], act_lo[:, j, 0:w],
                                             j == 0, j == FC - 1)
                            ins.then_inc(tile_used, 1)
                        if q:
                            x_sum(update, halves, i, q - 1)
                close_x_sums(update, halves)

            def project(stage, name=None):
                tiles = PROJ[stage]
                t0 = FIRST[stage]
                if name:
                    first_products(name, [proj_bank(k) for k in range(AHEAD)], t0, tiles[0]["halves"])
                for k in range(len(tiles) + 2):
                    if k < len(tiles) and not (name and k < AHEAD):
                        if k >= 3:
                            pe.wait_ge(of(stage, "evac_ready"), k - 2)
                            if tiles[k - 3]["kind"] == "n":
                                pe.wait_ge(of(stage, "sq_ready"), tiles[k - 3]["y"])
                        if stage == "proj_c" and k == 4:
                            pe.wait_ge(hl_ready, norm_done("mix_c"))
                        product(proj_bank(k), t0 + k, tiles[k]["halves"])
                    if 1 <= k <= len(tiles) and tiles[k - 1]["kind"] == "n":
                        y, w = tiles[k - 1]["y"], width(tiles[k - 1]["halves"])
                        pe.wait_ge(of(stage, "sq_ready"), y)
                        if y > 2:
                            pe.wait_ge(of(stage, "rs_ready"), y - 2)
                        nc.tensor.matmul(bank[2 + y % 2][:, 0:w], ones_head, stage_sq[:, y % 2, 0:w], start=True,
                                         stop=True).then_inc(of(stage, "ss_ready"), 1)
                    if k < 2:
                        continue
                    t = tiles[k - 2]
                    if t["kind"] == "n" and not t["rope"]:
                        continue
                    y, z, w = t["y"], t["z"], width(t["halves"])
                    if z > 2:
                        pe.wait_ge(of(stage, "z_ready"), z - 2)
                    to = bank[4 + z % 2]
                    if t["kind"] == "n":
                        pe.wait_ge(of(stage, "y_ready"), y)
                        ins = nc.tensor.matmul(to[:, 0:w], rot, stage_y[:, y % 2, 0:w], start=True, stop=True)
                    elif t["kind"] == "v":
                        pe.wait_ge(of(stage, "evac_ready"), k - 1)
                        for b in range(w // P):
                            ins = nc.tensor.transpose(to[:, b * P:(b + 1) * P],
                                                      stage_raw[:, (k - 2) % 2, b * P:(b + 1) * P], ident)
                    else:
                        pe.wait_ge(of(stage, "evac_ready"), k - 1)
                        if z == 1:
                            pe.wait_ge(table_loaded, 96)
                        for b in range(2):
                            ins = nc.tensor.matmul(to[:, b * P:(b + 1) * P],
                                                   stage_raw[:, (k - 2) % 2, b * P:(b + 1) * P], sub[:, t["c"], :],
                                                   start=True, stop=True)
                    ins.then_inc(of(stage, "rot_ready"), 1)

            def attend(pair):
                plan = PAIRS[pair]
                units, per, stage = plan["units"], plan["per"], plan["proj"]
                diff = pair == "pair_a"
                last = PROJ[stage][-1]
                if last["y"]:
                    pe.wait_ge(of(stage, "y_ready"), last["y"])
                pe.wait_ge(of(stage, "z_ready"), last["z"])
                q_of = Qc if pair == "pair_c" else Q

                def scores(u):
                    p, q = units[u]
                    lo, hi = unit_keys(pair, q)
                    if u >= 2:
                        pe.wait_ge(of(pair, "p_ready" if diff else "max_ready"), u - 1)
                    for c in range(2):
                        rows = slice(HEAD * c, HEAD * (c + 1))
                        keys = {"pair_a": K, "pair_b": K, "pair_c": Kc}[pair][rows, p // 2 if pair == "pair_b" else p,
                                                                              lo:hi]
                        ins = nc.tensor.matmul(bank[2 * (u % 2) + c][:, 0:hi - lo], q_of[rows, p, q * P:(q + 1) * P], keys,
                                               start=True, stop=True)
                    ins.then_inc(of(pair, "s_ready"), 1)

                def transposes(u):
                    p, q = units[u]
                    lo, hi = unit_keys(pair, q)
                    pe.wait_ge(of(pair, "w_ready"), u + 1)
                    if u >= 1:
                        pe.wait_ge(of(pair, "pT_ready"), u)
                    for c in range(1 if diff else 2):
                        for b in range((hi - lo) // P):
                            ins = nc.tensor.transpose(bank[4 + c][:, b * P:(b + 1) * P],
                                                      probs[:, u % 3, c, b * P:(b + 1) * P], ident)
                    ins.then_inc(of(pair, "tr_ready"), 1)

                def values(p):
                    pe.wait_ge(of(pair, "pT_ready"), per * (p + 1))
                    if pair == "pair_b":
                        if p >= 1:
                            pe.wait_ge(of(pair, "ol_ready"), p)
                        g = ada_after(pair, per * (p + 1) + LAG, 3)
                        if g is not None:
                            pe.wait_ge(mod_stored, g + 1)
                    elif p >= (1 if diff else 2):
                        pe.wait_ge(of(pair, "o_ready"), p if diff else p - 1)
                    to = value_bank(pair, p)
                    if diff:
                        t = pT[:, p % 2, :].rearrange("p (k q) -> p k q", k=4)
                        for half, first in ((0, 0), (1, 2)):
                            for k in range(first, 4):
                                ins = nc.tensor.matmul(to[:, half * NT:(half + 1) * NT], V[:, k, p * P:(p + 1) * P],
                                                       t[:, k, half * NT:(half + 1) * NT], start=k == first, stop=k == 3)
                    else:
                        nk = 4 if pair == "pair_b" else 2
                        for c in range(2):
                            t = pT[:, p % 2, c * D:c * D + nk * NT].rearrange("p (k q) -> p k q", k=nk)
                            for k in range(nk):
                                at = (p // 2) * HEAD if pair == "pair_b" else (2 * p + c) * HEAD
                                v = (V if pair == "pair_b" else Vc)[:, k, at:at + HEAD]
                                ins = nc.tensor.matmul(to[HEAD * c:HEAD * (c + 1), 0:NT], v, t[:, k, :], start=k == 0,
                                                       stop=k == nk - 1)
                    ins.then_inc(of(pair, "pv_ready"), 1)

                for u in range(len(units) + LAG + 1):
                    if u < len(units):
                        scores(u)
                    if u > LAG and (u - LAG) % per == 0:
                        values((u - LAG) // per - 1)
                    if LAG <= u < len(units) + LAG:
                        transposes(u - LAG)
                    g = ada_after(pair, u, 2)
                    if g is not None:
                        if pair == "pair_b" and u - LAG > per:
                            pe.wait_ge(of(pair, "ol_ready"), (u - LAG) // per)
                        ada_turn(g)
                    g = ada_group(pair, u)
                    if g is not None:
                        ada_product(g, ada_half(u))

            def project_out(stage, halves, update, name=None):
                t0 = FIRST[stage]
                if name:
                    first_products(name, bank[4:4 + AHEAD], t0, halves)
                    product(bank[7], t0 + AHEAD, halves)
                    open_x_sums()
                    for q in range(AHEAD):
                        x_sum(update, halves, 0, q)
                    for q in range(4):
                        product(bank[4 + q], t0 + 4 + q, halves)
                        if q:
                            x_sum(update, halves, 1, q - 1)
                else:
                    open_x_sums()
                    with pe.Fori(0, 2) as i:
                        for q in range(4):
                            product(bank[4 + q], t0 + q, halves, i, 4)
                            if q:
                                x_sum(update, halves, i, q - 1)
                close_x_sums(update, halves)

            pe.wait_ge(cs_ready, 3)

            for g in range(ADA_PART[0]):
                ada_product(g)
                if g >= 1:
                    ada_turn(g - 1)
                c = g - 3
                if 0 <= c < KC:
                    pe.wait_ge(mem_sq, c + 1)
                    nc.tensor.matmul(bank[1][:, 0:NT], ones, stage_z[:, c % 2, 0:NT], start=c == 0, stop=c == KC - 1
                                     ).then_inc(mem_sums, 1)
                    pe.wait_ge(sq_ready, c + 1)
                    nc.tensor.matmul(bank[0][:, :], ones, stage_sq[:, c % 2, :], start=c == 0, stop=c == KC - 1
                                     ).then_inc(sq_used, 1)
            ada_turn(ADA_PART[0] - 1)

            ffn(0, "pre0", "LC", 0)
            project("qkv_a", "mix_a")
            attend("pair_a")
            pe.wait_ge(mod_ready, 2)
            sums("sub_a")
            project_out("out_a", "LC", 1, "sub_a")
            ffn(1, "post0", "LC", 2)
            ffn(2, "pre1", "LC", 3)
            project("qkv_b", "mix_b")
            attend("pair_b")
            pe.wait_ge(of("pair_b", "ol_ready"), KC)
            project_out("out_b", "L", 4)
            ffn(3, "post1", "L", 5)
            pe.wait_ge(mem_split, 3)
            project("proj_c")
            attend("pair_c")
            sums("og_c")
            project_out("out_c", "L", 6, "og_c")
            project("peer_q", "ffn_c")

            t0 = FIRST["peer"]
            t1, t2 = t0 + EARLY_CHUNKS, t0 + 2 * EARLY_CHUNKS
            pe.wait_ge(of("peer_q", "z_ready"), PEER_ROWS)

            def early_up(i, q, first):
                if not (first and q < 2):
                    pe.wait_ge(of("peer", "gelu"), R * i + q - 1)
                product(bank[4 + q % 2], t0 + q, "L", i, R)

            for q in range(R):
                early_up(0, q, True)
            with pe.Fori(1, EARLY_CHUNKS // R) as i:
                for q in range(R):
                    early_up(i, q, False)

            pe.wait_ge(of("peer", "gelu"), EARLY_CHUNKS)

            pe.wait_ge(of("peer", "routed"), 1)
            for n in range(3):
                for t in range(2):
                    src = sel[:, n, t, :] if n < 2 else gate_tok[:, t, :]
                    ins = nc.tensor.transpose(bank[n][:, t * P:(t + 1) * P], src, ident)
                ins.then_inc(of("peer", "idx_tr"), 1)

            def spread(i, b, first):
                pe.wait_ge(of("peer", "gated"), 4 * i + b + 1)
                if not first:
                    pe.wait_ge(of("peer", "gates"), 4 * i + b - 3)
                for q in range(TOKENS_PER_GROUP):
                    ins = nc.tensor.matmul(bank[4 + b][:, q * P:(q + 1) * P], spread2[:, b, q, :], spread1[:, b, q, :],
                                           start=True, stop=True)
                ins.then_inc(of("peer", "spread"), 1)

            for b in range(4):
                spread(0, b, True)
            with pe.Fori(1, NT // TOKENS_PER_GROUP // 4) as i:
                for b in range(4):
                    spread(i, b, False)

            pe.wait_ge(of("peer", "idx_ready"), 3)
            for n in range(4):
                nc.tensor.matmul(bank[n][:, :], zeros[:, 0:P], zeros[:, :], start=True, stop=True)

            def up(t, b, i=0, per=0):
                product(bank[4 + b], t, "L", i, per)

            def down(t, c, b, i=0, per=0):
                pe.wait_ge(lo_ready, t + 1 + per * i)
                pe.wait_ge(of("peer", "w_lo"), c + 1)
                for m in range(KC):
                    ins = passes(bank[m // 2][:, (m % 2) * NT:(m % 2 + 1) * NT], t % R, m, pw_hi[:, b, :],
                                 pw_lo[:, b, :], False, True)
                ins.then_inc(tile_used, 1)

            with pe.Fori(0, EARLY_CHUNKS // R) as i:
                for q in range(R):
                    down(t1 + q, R * i + q, q % 2, i, R)
            for b in range(2):
                up(t2 + b, b)
            with pe.Fori(0, (EXPERT_CHUNKS - EARLY_CHUNKS) // 2 - 1) as i:
                for b in range(2):
                    c = EARLY_CHUNKS + 2 * i + b
                    pe.wait_ge(of("peer", "gelu"), c + 1)
                    up(t2 + 2 + 2 * b, b, i, 4)
                    down(t2 + 3 + 2 * b, c, b, i, 4)
            for b in range(2):
                down(N_TILES - 2 + b, EXPERT_CHUNKS - 2 + b, b)


def kernel(**inputs):
    import numpy as np
    import concourse.bacc as bacc
    from concourse.bass_utils import run_bass_kernel_spmd

    a = {k: np.asarray(v) for k, v in inputs.items()}
    f32 = np.float32

    def blocks(w):
        n = w.shape[1] // P
        return w.reshape(KC, P, n, P).transpose(2, 1, 0, 3).reshape(n, P, D)

    def ffn_in(w):
        n = w.shape[1] // 2
        return np.stack([blocks(w[:, :n]), blocks(w[:, n:])], 1).reshape(-1, P, D)

    def ffn_out(w):
        full = np.zeros((WO_T * D, D), f32)
        full[:FC * P] = w
        return full.reshape(WO_T, KC, P, KC, P).transpose(3, 0, 2, 1, 4).reshape(-1, P, D)

    def heads(w, *cuts):
        return blocks(np.concatenate([w[:, lo:hi] for lo, hi in cuts], 1))

    up = a["peer_u_2"][0].reshape(EXPERT_CHUNKS, P, KC, P).transpose(0, 3, 2, 1).reshape(-1, P, D)
    down = a["peer_v_2"][0].reshape(EXPERT_CHUNKS, P, D)
    first = EARLY_CHUNKS
    experts = [*up[:first], *down[:first], up[first], up[first + 1]]
    for c in range(first + 2, EXPERT_CHUNKS):
        experts += [up[c], down[c - 2]]
    experts += [down[-2], down[-1]]
    pre_i, pre_o, post_i, post_o = (a[k] for k in ("ffn_pre_wi", "ffn_pre_wo", "ffn_post_wi", "ffn_post_wo"))
    ada = a["ada_w"].reshape(2, ADA_TILES, 2, P, -1, 512).transpose(0, 4, 1, 3, 2, 5).reshape(-1, P, D)
    ada = np.split(ada, ADA_TILES * np.cumsum(ADA_PART)[:-1])
    w_stream = np.concatenate([
        ada[0], ffn_in(pre_i[0]), ffn_out(pre_o[0]), blocks(a["a_w_qkv"][0]), ada[1], blocks(a["a_w_o"][0]),
        ffn_in(post_i[0]), ffn_out(post_o[0]), ffn_in(pre_i[1]), ffn_out(pre_o[1]),
        heads(a["b_w_qkv"][0], (1024, 1536), (0, 1024)), ada[2], blocks(a["b_w_o"][0]),
        ffn_in(post_i[1]), ffn_out(post_o[1]),
        blocks(a["w_mem_kv_2"][0]), blocks(a["w_in_2"][0]), blocks(a["w_out_2"][0]),
        blocks(a["w_peer_q_2"][0]), np.stack(experts)])
    assert w_stream.shape[0] == N_TILES

    def tokens(x):
        return x.T.reshape(KC, P, -1).transpose(1, 0, 2)

    def col(v):
        return v.reshape(-1, P).T

    def row(v):
        return np.broadcast_to(v.reshape(1, -1), (P, v.size))

    def twice(name):
        return col(np.concatenate([a[name].reshape(-1)] * 2))

    small = dict(
        a_q=twice("a_q_gain"), a_k=twice("a_k_gain"), a_sub=col(a["a_subln_gain"]), b_q=twice("b_q_gain"),
        b_k=twice("b_k_gain"), dil_q=twice("qg_dil_2"), dil_k=twice("kg_dil_2"), moba_q=twice("qg_moba_2"),
        moba_k=twice("kg_moba_2"), mem_q=twice("qg_mem_2"), mem_k=twice("kg_mem_2"), g_mix=col(a["g_mix_2"]),
        g_mem=col(a["g_memtok_2"]),
        og=np.concatenate([col(a[k]) for k in ("og_dil_2", "og_moba_2", "og_mem_2")], 1), g_ffn=col(a["g_ffn_2"]),
        one=np.ones((P, 1), f32), pick=np.tile(np.eye(1, 2 * KC - 1, KC - 1, dtype=f32), (P, 1)), sink=row(a["b_sink"]), lam=row(a["a_lambda"]),
        c=np.stack([col(a["c"]), col(a["c_ctx"])], 2).reshape(P, -1), ada_b=col(a["ada_b"]))
    small = np.concatenate([small[k] for k in SMALL], 1)
    assert small.shape[1] == N_SMALL

    turn = np.zeros((P, P), f32)
    for d in range(P):
        turn[d + 16 if d % 32 < 16 else d - 16, d] = -1.0 if d % 32 < 16 else 1.0
    consts = np.stack([np.eye(P, dtype=f32), np.ones((P, P), f32), np.kron(np.eye(2), np.ones((HEAD, HEAD))).astype(f32),
                       turn], 1)
    inv = np.power(f32(10000.0), -np.arange(16, dtype=f32) / f32(16)).astype(f32)
    pos = np.arange(NT)
    ang = np.stack([(pos // 64).astype(f32)[:, None] * inv, (pos % 64).astype(f32)[:, None] * inv], 1)
    ang = np.stack([ang, ang], 2).reshape(NT, HEAD).T
    rope = np.zeros((P, 2, 2 * NT), f32)
    rope[:, 0, NT:] = 1.0
    rope[:, 0, :NT] = np.tile(np.cos(ang), (2, 1))
    rope[:, 1, :NT] = np.tile(np.sin(ang), (2, 1))
    qi, kj = pos[:, None], pos[None, :]
    mask = np.zeros((NT, 2 * NT), f32)
    mask[:, :NT] = np.where(np.abs(qi - kj) <= 128, 0.0, NEG)
    mask = mask.reshape(2, P, 2 * NT).transpose(1, 0, 2)
    dist = (qi - kj).astype(np.float64)
    count = ((dist >= 0) & (dist <= 128)).astype(int) + ((dist >= 0) & (dist % 4 == 0)) + ((dist >= 0) & (dist % 16 == 0))
    slopes = np.exp2(-8.0 * np.arange(1, 13) / 12)
    bias = np.zeros((12, NT, NT))
    for h in range(6):
        bias[h] = np.where(count > 0, (np.log(np.maximum(count, 1)) - slopes[2 * h] * dist) / SCALE, NEG)
        bias[6 + h] = np.where(dist >= 0, -slopes[2 * h + 1] * dist / SCALE, NEG)
    bias = bias.astype(f32).reshape(12, 2, P, NT).transpose(2, 0, 1, 3)
    subs = np.stack([a["peer_subkeys_1_2"][0], a["peer_subkeys_2_2"][0]], 1).reshape(PEER_ROWS, P, P).transpose(2, 0, 1)

    arrays = dict(
        w_stream=w_stream, x_in=np.stack([tokens(a["x"][0]), tokens(a["ctx"][0])], 1),
        mem_in=tokens(a["mem_2"][0]), small_in=small, const_in=consts, rope_in=rope, fan_in=np.kron(np.eye(KC), np.ones((1, P))).reshape(KC, KC, P), mask_in=mask, bias_in=bias,
        sub_in=subs)
    nc = bacc.Bacc("TRN2", target_bir_lowering=False, num_devices=1, dynamic_dma_scratch_size=1024)
    args = {}
    for name in arrays:
        arrays[name] = np.ascontiguousarray(arrays[name], dtype=f32)
        args[name] = nc.dram_tensor(f"{name}_dram", arrays[name].shape, F32, kind="ExternalInput").ap()
    args["gelu_dram"] = nc.dram_tensor("gelu_scratch", (EARLY_CHUNKS, P, NT), F32, kind="Internal").ap()
    args["out"] = nc.dram_tensor("out_dram", (P, KC, NT), F32, kind="ExternalOutput").ap()
    program(nc, **args)
    r = run_bass_kernel_spmd(nc, [{f"{k}_dram": v for k, v in arrays.items()}], core_ids=[0])
    got = np.asarray(r.results[0]["out_dram"])
    return got.transpose(2, 1, 0).reshape(1, NT, D)
```
